# Optimizing a Trainium2 kernel written in Bass

```python
import math
import jax, jax.numpy as jnp
from jax import lax
import numpy as np

D_MODEL = 1024
BATCH = 1
SEQ = 512
DEPTH = 2
DEC_BATCH = 1
DEC_SEQ = 64
PAST_LEN = 128

CHUNK = 64
D_MIX = D_MODEL
D_A = D_MIX // 2
D_B = D_MIX - D_A
HEAD_DIM = 64
N_HEADS_A = D_A // HEAD_DIM
N_KV_HEADS = 2
GQA_GROUP = N_HEADS_A // N_KV_HEADS
D_KV = N_KV_HEADS * HEAD_DIM
ROT_DIM = HEAD_DIM // 4
N_IDX_HEADS = 8
IDX_DIM = 32
IDX_ROT = IDX_DIM // 4
TOPK_MAX = 256
QBLK = 128
N_GROUPS_B = 8
GROUP_DIM_B = D_B // N_GROUPS_B
GMLP_CHUNK = 128
D_FF = 4 * D_MODEL
ROPE_THETA = 500000.0
EPS = 1e-6
N_IN = D_A + 2 * D_KV + N_IDX_HEADS * IDX_DIM + IDX_DIM + N_IDX_HEADS + 2 * D_B

kernel_name = 'hybrid_dsa_gmlp_stream_step'

def rmsnorm(x, g):
    xf = x.astype(jnp.float32)
    y = xf * lax.rsqrt(jnp.mean(xf * xf, axis=-1, keepdims=True) + EPS)
    return (y * g.astype(jnp.float32)).astype(x.dtype)

def rope(x, pos, rot):
    half = rot // 2
    inv = ROPE_THETA ** (-jnp.arange(half, dtype=jnp.float32) * (2.0 / rot))
    ang = pos.astype(jnp.float32)[:, None] * inv[None, :]
    cos = jnp.cos(ang)[None, :, None, :]
    sin = jnp.sin(ang)[None, :, None, :]
    xf = x.astype(jnp.float32)
    x1 = xf[..., :half]
    x2 = xf[..., half:rot]
    out = jnp.concatenate([x1 * cos - x2 * sin, x2 * cos + x1 * sin, xf[..., rot:]], axis=-1)
    return out.astype(x.dtype)

def chunk_mask(n, dtype):
    c = jnp.arange(n) // CHUNK
    return (c[None, :] <= c[:, None]).astype(dtype)

def project(xn, w_in, pos):
    B, T, _ = xn.shape
    z = xn @ w_in
    sizes = (D_A, D_KV, D_KV, N_IDX_HEADS * IDX_DIM, IDX_DIM, N_IDX_HEADS, D_B, D_B)
    parts = []
    off = 0
    for s in sizes:
        parts.append(z[..., off:off + s])
        off += s
    q, k, v, qi, ki, wi, u, gv = parts
    q = rope(q.reshape(B, T, N_HEADS_A, HEAD_DIM), pos, ROT_DIM)
    k = rope(k.reshape(B, T, N_KV_HEADS, HEAD_DIM), pos, ROT_DIM)
    v = v.reshape(B, T, N_KV_HEADS, HEAD_DIM)
    qi = rope(qi.reshape(B, T, N_IDX_HEADS, IDX_DIM), pos, IDX_ROT)
    ki = rope(ki.reshape(B, T, 1, IDX_DIM), pos, IDX_ROT)[:, :, 0]
    return q, k, v, qi, ki, wi, u, gv

def dsa_attend(q, qi, wi, pos_q, k, v, ki, pos_k, topk):
    B, Tq = q.shape[:2]
    rel = jax.nn.relu(jnp.einsum('bthd,bsd->bths', qi.astype(jnp.float32), ki.astype(jnp.float32)))
    score = jnp.einsum('bths,bth->bts', rel, wi.astype(jnp.float32)) * (IDX_DIM ** -0.5 * N_IDX_HEADS ** -0.5)
    admissible = (pos_k[None, :] // CHUNK) <= (pos_q[:, None] // CHUNK)
    score = jnp.where(admissible[None], score, -jnp.inf)
    top_val, top_idx = lax.top_k(score, topk)
    valid = jnp.isfinite(top_val)
    take_rows = jax.vmap(lambda a, idx: a[idx])
    k_sel = take_rows(k, top_idx)
    v_sel = take_rows(v, top_idx)
    qg = q.reshape(B, Tq, N_KV_HEADS, GQA_GROUP, HEAD_DIM)
    logits = jnp.einsum('btkgd,btskd->btkgs', qg, k_sel).astype(jnp.float32) * (HEAD_DIM ** -0.5)
    logits = jnp.where(valid[:, :, None, None, :], logits, -jnp.inf)
    p = jax.nn.softmax(logits, axis=-1).astype(v.dtype)
    o = jnp.einsum('btkgs,btskd->btkgd', p, v_sel)
    return o.reshape(B, Tq, D_A)

def dsa_prompt(q, qi, wi, k, v, ki, pos):
    B, T = q.shape[:2]
    nb = T // QBLK
    topk = min(TOPK_MAX, T // 4)

    def blocks(a):
        return jnp.swapaxes(a.reshape((B, nb, QBLK) + a.shape[2:]), 0, 1)

    out = lax.map(lambda args: dsa_attend(args[0], args[1], args[2], args[3], k, v, ki, pos, topk),
                  (blocks(q), blocks(qi), blocks(wi), pos.reshape(nb, QBLK)))
    return jnp.swapaxes(out, 0, 1).reshape(B, T, D_A)

def spatial_prompt(gvn, w_s, b_s):
    B, T, _ = gvn.shape
    n = T // GMLP_CHUNK
    vg = gvn.reshape(B, n, GMLP_CHUNK, N_GROUPS_B, GROUP_DIM_B)
    w = w_s * chunk_mask(GMLP_CHUNK, w_s.dtype)[None]
    mix = jnp.einsum('gij,bnjgc->bnigc', w, vg) + b_s.T[None, None, :, :, None]
    return mix.reshape(B, T, D_B)

def spatial_sample(gvn, w_s, b_s):
    B, Ts, _ = gvn.shape
    vg = gvn.reshape(B, Ts, N_GROUPS_B, GROUP_DIM_B)
    w = w_s[:, :Ts, :Ts] * chunk_mask(Ts, w_s.dtype)[None]
    mix = jnp.einsum('gij,bjgc->bigc', w, vg) + b_s[:, :Ts].T[None, :, :, None]
    return mix.reshape(B, Ts, D_B)

def sq_relu_ffn(x, w1, w2):
    h = jax.nn.relu(x @ w1)
    return (h * h) @ w2

def setup_inputs(seed: int = 0) -> dict:
    key = jax.random.key(seed)
    ks = jax.random.split(key, 16)
    f32 = jnp.float32
    nrm = lambda k, shape, scale: jax.random.normal(k, shape, f32) * scale
    return {
        'x_prompt': nrm(ks[0], (BATCH, SEQ, D_MODEL), 1.0),
        'x_sample': nrm(ks[1], (DEC_BATCH, DEC_SEQ, D_MODEL), 1.0),
        'cache_k': nrm(ks[2], (DEPTH, DEC_BATCH, PAST_LEN, N_KV_HEADS, HEAD_DIM), 1.0),
        'cache_v': nrm(ks[3], (DEPTH, DEC_BATCH, PAST_LEN, N_KV_HEADS, HEAD_DIM), 1.0),
        'cache_kidx': nrm(ks[4], (DEPTH, DEC_BATCH, PAST_LEN, IDX_DIM), 1.0),
        'norm_mix': 1.0 + nrm(ks[5], (DEPTH, D_MODEL), 0.02),
        'w_in': nrm(ks[6], (DEPTH, D_MODEL, N_IN), D_MODEL ** -0.5),
        'gate_norm': 1.0 + nrm(ks[7], (DEPTH, D_B), 0.02),
        'w_spatial': nrm(ks[8], (DEPTH, N_GROUPS_B, GMLP_CHUNK, GMLP_CHUNK), GMLP_CHUNK ** -0.5),
        'b_spatial': 1.0 + nrm(ks[9], (DEPTH, N_GROUPS_B, GMLP_CHUNK), 0.02),
        'w_out': nrm(ks[10], (DEPTH, D_MIX, D_MODEL), D_MIX ** -0.5),
        'norm_ffn': 1.0 + nrm(ks[11], (DEPTH, D_MODEL), 0.02),
        'w_ff1': nrm(ks[12], (DEPTH, D_MODEL, D_FF), D_MODEL ** -0.5),
        'w_ff2': nrm(ks[13], (DEPTH, D_FF, D_MODEL), D_FF ** -0.5),
        'norm_final': 1.0 + nrm(ks[14], (D_MODEL,), 0.02),
    }

def reference(x_prompt, x_sample, cache_k, cache_v, cache_kidx, norm_mix, w_in, gate_norm,
              w_spatial, b_spatial, w_out, norm_ffn, w_ff1, w_ff2, norm_final):
    T = x_prompt.shape[1]
    Ts = x_sample.shape[1]
    past = cache_k.shape[2]
    pos_p = jnp.arange(T, dtype=jnp.int32)
    pos_s = past + jnp.arange(Ts, dtype=jnp.int32)
    pos_all = jnp.arange(past + Ts, dtype=jnp.int32)
    topk_s = min(TOPK_MAX, (past + Ts) // 4)

    xp = x_prompt
    xs = x_sample
    kp_l, vp_l, kip_l, ks_l, vs_l, kis_l, gvs_l = [], [], [], [], [], [], []
    for l in range(DEPTH):
        xn = rmsnorm(xp, norm_mix[l])
        q, k, v, qi, ki, wi, u, gv = project(xn, w_in[l], pos_p)
        a = dsa_prompt(q, qi, wi, k, v, ki, pos_p)
        gvn = rmsnorm(jax.nn.gelu(gv), gate_norm[l])
        bmix = jax.nn.gelu(u) * spatial_prompt(gvn, w_spatial[l], b_spatial[l])
        xp = xp + jnp.concatenate([a, bmix], axis=-1) @ w_out[l]
        xp = xp + sq_relu_ffn(rmsnorm(xp, norm_ffn[l]), w_ff1[l], w_ff2[l])
        kp_l.append(k)
        vp_l.append(v)
        kip_l.append(ki)

        xn = rmsnorm(xs, norm_mix[l])
        q, k, v, qi, ki, wi, u, gv = project(xn, w_in[l], pos_s)
        k_all = jnp.concatenate([cache_k[l], k], axis=1)
        v_all = jnp.concatenate([cache_v[l], v], axis=1)
        ki_all = jnp.concatenate([cache_kidx[l], ki], axis=1)
        a = dsa_attend(q, qi, wi, pos_s, k_all, v_all, ki_all, pos_all, topk_s)
        gvn = rmsnorm(jax.nn.gelu(gv), gate_norm[l])
        bmix = jax.nn.gelu(u) * spatial_sample(gvn, w_spatial[l], b_spatial[l])
        xs = xs + jnp.concatenate([a, bmix], axis=-1) @ w_out[l]
        xs = xs + sq_relu_ffn(rmsnorm(xs, norm_ffn[l]), w_ff1[l], w_ff2[l])
        ks_l.append(k)
        vs_l.append(v)
        kis_l.append(ki)
        gvs_l.append(gvn)

    y_prompt = rmsnorm(xp, norm_final)
    y_sample = rmsnorm(xs, norm_final)
    k_prompt = jnp.stack(kp_l)
    v_prompt = jnp.stack(vp_l)
    kidx_prompt = jnp.stack(kip_l)
    k_sample = jnp.stack(ks_l)
    v_sample = jnp.stack(vs_l)
    kidx_sample = jnp.stack(kis_l)
    gv_sample = jnp.stack(gvs_l)
    return (y_prompt, y_sample, k_prompt, v_prompt, kidx_prompt, k_sample, v_sample, kidx_sample, gv_sample)


_drawn_inputs = setup_inputs


def setup_inputs(seed=0):
    import zlib

    import numpy as np

    out = dict(_drawn_inputs(seed))
    spreads = {}
    factors = {'gate_norm': 7.555, 'b_spatial': 4.034, 'norm_final': 8.225, 'norm_ffn': 3.774}
    for name, (base, spread) in spreads.items():
        noise = np.random.default_rng([zlib.crc32(name.encode()), seed]).standard_normal(out[name].shape)
        drawn = base * np.exp(spread * noise) if base else spread * noise
        out[name] = __import__('jax').numpy.asarray(drawn.astype(out[name].dtype))
    for name, factor in factors.items():
        out[name] = (out[name] * factor).astype(out[name].dtype)
    return out
```

```python
import concourse.bass as bass
from concourse import mybir
from contextlib import ExitStack


def hybrid_encoder_program(nc, A, O):
    F32 = mybir.dt.float32
    ALU = mybir.AluOpType
    ACT = mybir.ActivationFunctionType

    P = 128
    SEQ, D = A["x_prompt"].shape[1], A["x_prompt"].shape[2]
    DEC = A["x_sample"].shape[1]
    DEPTH, _, PAST, NKV, HD = A["cache_k"].shape
    ID = A["cache_kidx"].shape[3]
    N_IN = A["w_in"].shape[2]
    DB = A["gate_norm"].shape[1]
    NG = A["w_spatial"].shape[1]
    DFF = A["w_ff1"].shape[2]
    DA = D - DB
    NH = DA // HD
    NIH = 8
    CHUNK = 64
    KT = D // P
    FT = DFF // P
    CPG = DB // NG
    DKV = NKV * HD
    TOP_P, TOP_S = min(256, SEQ // 4), min(256, (PAST + DEC) // 4)
    EPS = 1e-6
    NPT = SEQ // P
    NT = NPT + 1
    SMP = NPT
    TOK = SEQ + DEC
    HALF = TOK // 2
    ROWS = [P] * NPT + [DEC]
    KEYS = [P * (t + 1) for t in range(NPT)] + [PAST + DEC]
    RH, RI = HD // 8, ID // 8
    NEG, TAKEN, SPLIT, OFF = -2e38, -3e38, -2.5e38, -1e30
    SCALE = float(HD) ** -0.5

    C_Q, C_K = 0, DA
    C_SMALL = DA + 2 * DKV + NIH * ID
    NSM = ID + NIH
    C_U = C_SMALL + NSM
    C_GV = C_U + DB
    CW = 512
    CHUNKS = [C_K, C_Q, C_GV, C_U]
    KVQI, QQ, GV, UU = range(4)
    ZW = CW + NSM
    Z_K, Z_V, Z_QI, Z_KI, Z_WI = 0, DKV, 2 * DKV, CW, CW + ID

    NSLOT = 4
    PW = 256
    NPAIR = D // PW
    F1_ROUNDS = DFF // PW // NSLOT
    F2_ROUNDS = NPAIR
    S_OUT = 2 * len(CHUNKS)
    S_F1 = S_OUT + NPAIR
    S_F2 = S_F1 + DFF // PW
    SLOTS = S_F2 + NPAIR * NSLOT

    TILE_ORDER = [0, SMP] + list(range(1, NPT))
    ITEMS = [(t, h) for t in TILE_ORDER for h in range(NH)]
    NI = len(ITEMS)
    INDEX_TILES = [SMP] + list(range(1, NPT))
    INDEX = [(t, h) for t in INDEX_TILES for h in range(NIH)]
    NX = len(INDEX)

    def cols(t):
        return slice(t * P, t * P + ROWS[t])

    ctx = ExitStack()
    with ctx:
        def sb(name, shape, dt=F32):
            return ctx.enter_context(nc.sbuf_tensor(name, shape, dt))

        def sem(name):
            return ctx.enter_context(nc.semaphore(name))

        x = sb("x", [P, KT, TOK])
        xg = sb("xg", [P, KT, TOK])
        ring = sb("ring", [P, NSLOT, KT * PW])
        w_small = sb("w_small", [P, KT, NSM])
        ident = sb("ident", [P, P])
        ones = sb("ones", [P, P])
        grow = sb("grow", [7 * KT, P])
        gcol = sb("gcol", [P, 7 * KT])
        rope_t = sb("rope_t", [P, NT, 4 * RH + 4 * RI])
        w_sp = sb("w_sp", [P, NG, P])
        w_spT = sb("w_spT", [P, NG, P])
        gate_bc = sb("gate_bc", [P, DB])
        cache_k = sb("cache_k_t", [P, DKV])
        cache_v = sb("cache_v_t", [P, DKV])
        cache_ki = sb("cache_ki_t", [P, ID])
        cache_ki4 = sb("cache_ki4", [P, 4, ID])
        ssacc = sb("ssacc", [P, NT * P])
        sq = sb("sq", [P, 2, TOK])
        rl2 = sb("rl2", [P, 2, TOK])
        r2b = sb("r2b", [P, TOK])
        yb = sb("yb", [P, 2, TOK])
        ms = sb("ms", [P, NT])
        r = sb("r", [P, NT])
        ssv = sb("ssv", [P, NT])
        rv = sb("rv", [P, NT])
        mv = sb("mv", [P, NT])
        nw = sb("nw", [P, NT])
        wi = sb("wi", [P, NT, NIH])
        m8 = sb("m8", [P, 2, 8])
        mask0 = sb("mask0", [P, P])
        nmax = sb("nmax", [P, NI])
        rsum = sb("rsum", [P, NI])
        rinv = sb("rinv", [P, NI])
        z = sb("z", [P, NT, ZW])

        work = sb("work", [P, 22720])
        used = [0]

        def take(*dims):
            n = 1
            for d in dims:
                n *= d
            v = work[:, used[0]:used[0] + n]
            used[0] += n
            if len(dims) == 1:
                return v
            if len(dims) == 2:
                return v.rearrange("p (a b) -> p a b", a=dims[0])
            return v.rearrange("p (a b c) -> p a b c", a=dims[0], b=dims[1])

        h = work[:, 0:FT * TOK].rearrange("p (f n) -> p f n", f=FT)
        x_in = work[:, 0:NT * D].rearrange("p (t n) -> p t n", t=NT)
        out_b = work[:, 0:NT * D].rearrange("p (t n) -> p t n", t=NT)
        q = take(NT, DA)
        mixT = take(KT, TOK)
        ug = take(NT, DB)
        gvn = take(NT, DB)
        kT = take(SEQ)
        kTs = take(PAST + DEC)
        kiT = take(SEQ)
        kiTs = take(PAST + DEC)
        ki4 = take(NT, 4 * ID)
        qiT = take(2, TOK)
        score = {t: take(KEYS[t]) for t in INDEX_TILES}
        qT = take(4, TOK)
        rl = take(3, SEQ)
        L = rl
        pr = take(2, SEQ)
        pT = take(2, SEQ)
        rope_w = NT * NH * 2 * RH
        ra, rb = (mixT[:, :, :].rearrange("p k n -> p (k n)")[:, i * rope_w:(i + 1) * rope_w]
                  .rearrange("p (t n) -> p t n", t=NT) for i in range(2))
        mb = sq[:, :, 0:DB]
        o = rl2[:, :, 0:DA]
        assert used[0] <= 22720, used

        bank = [ctx.enter_context(nc.psum_tensor(f"bank{i}", [P, 512], F32)) for i in range(8)]

        w_ready = [sem(f"w_ready{s}") for s in range(NSLOT)]
        half_done = sem("half_done")
        const_in = sem("const_in")
        x_loaded = sem("x_loaded")
        small_in = sem("small_in")
        ws_in = sem("ws_in")
        const_made = sem("const_made")
        layer_buf_free = sem("layer_buf_free")
        xT_done, xT_evac = sem("xT_done"), sem("xT_evac")
        gT_done, g_ready = sem("gT_done"), sem("g_ready")
        x_ready = sem("x_ready")
        sq_ready, ss_added = sem("sq_ready"), sem("ss_added")
        xg_ready = sem("xg_ready")
        ss_done, ms_ready, r_ready = sem("ss_done"), sem("ms_ready"), sem("r_ready")
        root_ready, mv_ready = sem("root_ready"), sem("mv_ready")
        proj_done, proj_evac = sem("proj_done"), sem("proj_evac")
        small_done, small_evac = sem("small_done"), sem("small_evac")
        roped, q_roped = sem("roped"), sem("q_roped")
        tr_done, tr_evac = sem("tr_done"), sem("tr_evac")
        idx_done, idx_relu, idx_acc = sem("idx_done"), sem("idx_relu"), sem("idx_acc")
        gv_sq, rv_ready, gvn_ready = sem("gv_sq"), sem("rv_ready"), sem("gvn_ready")
        mix_done, mix_evac, bm_ready = sem("mix_done"), sem("mix_evac"), sem("bm_ready")
        qk_done, masked, exp_done = sem("qk_done"), sem("masked"), sem("exp_done")
        pT_done, pT_evac = sem("pT_done"), sem("pT_evac")
        o_ready = sem("o_ready")
        mt_done, mt_evac = sem("mt_done"), sem("mt_evac")
        out_done = sem("out_done")
        o_item, spT_ready, y_ready = sem("o_item"), sem("spT_ready"), sem("y_ready")
        ssb_done, ssb_read = sem("ssb_done"), sem("ssb_read")
        f1_done, f1_relu, h_ready = sem("f1_done"), sem("f1_relu"), sem("h_ready")
        f2_done = sem("f2_done")
        fin_done, fin_evac = sem("fin_done"), sem("fin_evac")
        dve_step, pool_step = sem("dve_step"), sem("pool_step")
        kv_out = sem("kv_out")
        y_out = sem("y_out")

        block = ctx.enter_context(nc.Block())

        NTR1 = 6
        NTR = NTR1 + 5
        KV_OUTS = 7

        def index_after(c, half, t):
            if c < GV:
                return []
            n = ((c - GV) * 2 + half) * NT + t
            return [i for i in range(2 * n, min(2 * n + 2, NX))]

        def last_reader(n):
            l, n = n // SLOTS, n % SLOTS
            if n < S_OUT:
                return (proj_done, NT * (4 * l + n // 2 + 1)) if n % 2 else (half_done, 16 * l + n // 2 + 1)
            if n < S_F1:
                return out_done, KT * l + 2 * (n - S_OUT + 1)
            if n < S_F2:
                return f1_done, FT * l + 2 * (n - S_F1 + 1)
            j, m = divmod(n - S_F2, NSLOT)
            return (half_done, 16 * l + 4 + 3 * j + m + 1) if m < NSLOT - 1 else (f2_done, KT * l + 2 * (j + 1))

        @block.sync
        def _(sp):
            sp.dma_start(x_in[:, 0:NPT, :], A["x_prompt"][0].rearrange("(t p) d -> p t d", p=P)).then_inc(x_loaded, 16)
            sp.dma_start(x_in[0:DEC, SMP, :], A["x_sample"][0]).then_inc(x_loaded, 16)
            row = 0
            for src in (A["norm_mix"], A["norm_ffn"], A["norm_final"], A["b_spatial"]):
                v = src.rearrange("l (k p) -> (l k) p", p=P) if len(src.shape) == 2 else (
                    src.rearrange("(k p) -> k p", p=P) if len(src.shape) == 1 else src.rearrange("l g p -> (l g) p"))
                sp.dma_start(grow[row:row + v.shape[0], :], v).then_inc(const_in, 16)
                row += v.shape[0]
            sp.dma_start(rope_t[:, :, :], A["rope_table"]).then_inc(const_in, 16)
            for l in range(DEPTH):
                n = [0]

                def load(src, runs):
                    s, use = n[0] % NSLOT, l * (SLOTS // NSLOT) + n[0] // NSLOT
                    if use:
                        sp.wait_ge(*last_reader(l * SLOTS + n[0] - NSLOT))
                    sp.dma_start(ring[:, s, :].rearrange("p (k n) -> p k n", k=runs), src).then_inc(w_ready[s], 16)
                    n[0] += 1

                if l:
                    sp.wait_ge(layer_buf_free, l)
                sp.dma_start(w_small[:, :, :], A["w_in"][l, :, C_SMALL:C_SMALL + NSM]
                             .rearrange("(k p) n -> p k n", p=P)).then_inc(ws_in, 16)
                for c, c0 in enumerate(CHUNKS):
                    for half in range(2):
                        load(A["w_in"][l, half * D // 2:(half + 1) * D // 2, c0:c0 + CW]
                             .rearrange("(k p) n -> p k n", p=P), KT // 2)
                    if c == 0:
                        sp.dma_start(cache_k[:, :], A["cache_k"][l, 0].rearrange("s h d -> s (h d)")).then_inc(small_in, 16)
                        sp.dma_start(cache_v[:, :], A["cache_v"][l, 0].rearrange("s h d -> s (h d)")).then_inc(small_in, 16)
                        sp.dma_start(cache_ki[:, :], A["cache_kidx"][l, 0]).then_inc(small_in, 16)
                        sp.dma_start(w_sp[:, :, :], A["w_spatial"][l].rearrange("g i j -> i g j")).then_inc(small_in, 16)
                        sp.dma_start(gate_bc[:, :], A["gate_norm"][l:l + 1, :].partition_broadcast(P) if False else
                                     A["gate_norm"][l:l + 1, :].broadcast_to([P, DB])).then_inc(small_in, 16)
                for p_ in range(NPAIR):
                    load(A["w_out"][l, :, p_ * PW:(p_ + 1) * PW].rearrange("(k p) n -> p k n", p=P), KT)
                    if p_ == 0:
                        sp.wait_ge(roped, l + 1)
                        zp = z[:, 0:NPT, :]
                        zs = z[0:DEC, SMP, :]
                        sp.dma_start(O["k_prompt"][l, 0].rearrange("(t p) h d -> p t (h d)", p=P), zp[:, :, Z_K:Z_K + DKV]).then_inc(kv_out, 16)
                        sp.dma_start(O["v_prompt"][l, 0].rearrange("(t p) h d -> p t (h d)", p=P), zp[:, :, Z_V:Z_V + DKV]).then_inc(kv_out, 16)
                        sp.dma_start(O["kidx_prompt"][l, 0].rearrange("(t p) d -> p t d", p=P), zp[:, :, Z_KI:Z_KI + ID]).then_inc(kv_out, 16)
                        sp.dma_start(O["k_sample"][l, 0].rearrange("p h d -> p (h d)"), zs[:, Z_K:Z_K + DKV]).then_inc(kv_out, 16)
                        sp.dma_start(O["v_sample"][l, 0].rearrange("p h d -> p (h d)"), zs[:, Z_V:Z_V + DKV]).then_inc(kv_out, 16)
                        sp.dma_start(O["kidx_sample"][l, 0], zs[:, Z_KI:Z_KI + ID]).then_inc(kv_out, 16)
                        sp.wait_ge(gvn_ready, NT * l + NT)
                        sp.dma_start(O["gv_sample"][l, 0], gvn[0:DEC, SMP, :]).then_inc(kv_out, 16)
                for i in range(DFF // PW):
                    load(A["w_ff1"][l, :, i * PW:(i + 1) * PW].rearrange("(k p) n -> p k n", p=P), KT)
                for j in range(NPAIR):
                    for m in range(NSLOT):
                        load(A["w_ff2"][l, m * D:(m + 1) * D, j * PW:(j + 1) * PW].rearrange("(k p) n -> p k n", p=P), KT)
            for t in range(NT):
                sp.wait_ge(fin_evac, 2 * t + 2)
                dst = O["y_prompt"][0, t * P:(t + 1) * P, :] if t < NPT else O["y_sample"][0]
                sp.dma_start(dst, out_b[0:ROWS[t], t, :]).then_inc(y_out, 16)
            sp.wait_ge(y_out, 16 * NT)
            sp.wait_ge(kv_out, 16 * KV_OUTS * DEPTH)

        @block.gpsimd
        def _(pool):
            count = [0]

            def link(ins):
                count[0] += 1
                ins.then_inc(pool_step, 1)
                pool.wait_ge(pool_step, count[0])

            g = nc.gpsimd
            link(g.memset(ident[:, :], 0.0))
            g.affine_select(out=ident[:, :], in_=ident[:, :], compare_op=ALU.not_equal, fill=1.0, base=0,
                            pattern=[[-1, P]], channel_multiplier=1).then_inc(const_made, 1)
            g.memset(ones[:, :], 1.0).then_inc(const_made, 1)
            g.memset(ssacc[:, TOK:NT * P], 0.0).then_inc(const_made, 1)
            g.memset(ssv[:, :], 1.0).then_inc(const_made, 1)
            link(g.memset(mask0[:, :], 0.0))
            g.memset(mask0[0:CHUNK, CHUNK:P], OFF).then_inc(const_made, 1)

            def sum_squares(base):
                for j in range(KT):
                    pool.wait_ge(sq_ready, base + j + 1)
                    if j == 0:
                        ins = g.tensor_copy(ssacc[:, 0:TOK], sq[:, j % 2, :])
                    else:
                        pool.wait_ge(ss_added, base + j)
                        ins = g.tensor_tensor(ssacc[:, 0:TOK], ssacc[:, 0:TOK], sq[:, j % 2, :], ALU.add)
                    ins.then_inc(ss_added, 1)

            def newton(y, m):
                link(g.tensor_tensor(nw[:, :], y[:, :], y[:, :], ALU.mult))
                link(g.tensor_tensor(nw[:, :], nw[:, :], m[:, :], ALU.mult))
                link(g.tensor_scalar(nw[:, :], nw[:, :], -0.5, 1.5, ALU.mult, ALU.add))

            def rope(buf, base, heads, width, half, rows, ts, table):
                nt = ts.stop - ts.start
                v = buf[0:rows, ts, base:base + heads * width].rearrange("p t (h d) -> p t h d", h=heads)
                ta = ra[0:rows, ts, 0:heads * 2 * half].rearrange("p t (h d) -> p t h d", h=heads)
                tb = rb[0:rows, ts, 0:heads * 2 * half].rearrange("p t (h d) -> p t h d", h=heads)

                def tab(a, b):
                    return rope_t[0:rows, ts, table + a:table + b].rearrange("p t (o d) -> p t o d", o=1)\
                        .broadcast_to([rows, nt, heads, b - a])
                g.tensor_tensor(ta, v[:, :, :, 0:2 * half], tab(0, 2 * half), ALU.mult)
                g.tensor_tensor(tb[:, :, :, 0:half], v[:, :, :, half:2 * half], tab(2 * half, 3 * half), ALU.mult)
                link(g.tensor_tensor(tb[:, :, :, half:2 * half], v[:, :, :, 0:half], tab(3 * half, 4 * half), ALU.mult))
                link(g.tensor_tensor(v[:, :, :, 0:2 * half], ta, tb, ALU.add))

            parts = [(P, slice(0, NPT)), (DEC, slice(SMP, NT))]
            sum_squares(0)
            for l in range(DEPTH):
                pool.wait_ge(root_ready, 2 * l + 1)
                newton(r, ms)
                g.tensor_tensor(r[:, :], r[:, :], nw[:, :], ALU.mult).then_inc(r_ready, 1)
                pool.wait_ge(small_in, 16 * 5 * (l + 1))
                g.tensor_copy(cache_ki4[:, :, :], cache_ki[:, :].rearrange("p (o d) -> p o d", o=1).broadcast_to([P, 4, ID]))
                pool.wait_ge(const_in, 16 * 5)
                pool.wait_ge(small_evac, l + 1)
                pool.wait_ge(proj_evac, 4 * NT * l + NT)
                for rows, ts in parts:
                    rope(z, Z_K, NKV, HD, RH, rows, ts, 0)
                    rope(z, Z_QI, NIH + 1, ID, RI, rows, ts, 4 * RH)
                for rows, ts in parts:
                    g.tensor_copy(ki4[0:rows, ts, :].rearrange("p t (o d) -> p t o d", o=4),
                                  z[0:rows, ts, Z_KI:Z_KI + ID].rearrange("p t (o d) -> p t o d", o=1)
                                  .broadcast_to([rows, ts.stop - ts.start, 4, ID]))
                    last = g.tensor_scalar(wi[0:rows, ts, :], z[0:rows, ts, Z_WI:Z_WI + NIH],
                                           float(ID) ** -0.5 * float(NIH) ** -0.5, None, ALU.mult)
                last.then_inc(roped, 1)
                pool.wait_ge(proj_evac, 4 * NT * l + 2 * NT)
                for rows, ts in parts:
                    rope(q, 0, NH, HD, RH, rows, ts, 0)
                g.memset(m8[:, 0, :], 0.0).then_inc(q_roped, 1)
                pool.wait_ge(root_ready, 2 * l + 2)
                newton(rv, mv)
                g.tensor_tensor(rv[:, :], rv[:, :], nw[:, :], ALU.mult).then_inc(rv_ready, 1)
                for a, t in enumerate(TILE_ORDER):
                    pool.wait_ge(proj_evac, 4 * NT * (l + 1))
                    pool.wait_ge(mix_evac, NT * l + a + 1)
                    g.tensor_tensor(ug[0:ROWS[t], t, :], ug[0:ROWS[t], t, :], mb[0:ROWS[t], a % 2, :], ALU.mult)\
                        .then_inc(bm_ready, 1)
                sum_squares(KT * (2 * l + 1))
                sum_squares(KT * (2 * l + 2))
            pool.wait_ge(root_ready, 2 * DEPTH + 1)
            newton(r, ms)
            g.tensor_tensor(r[:, :], r[:, :], nw[:, :], ALU.mult).then_inc(r_ready, 1)

        @block.scalar
        def _(act):
            s = nc.scalar

            def squares(base):
                for j in range(KT):
                    act.wait_ge(x_ready, base + j + 1)
                    if base + j >= 2:
                        act.wait_ge(ss_added, base + j - 1)
                    s.activation(sq[:, j % 2, :], x[:, j, :], ACT.Square).then_inc(sq_ready, 1)

            for t in range(NT):
                for half in range(2):
                    act.wait_ge(xT_done, 2 * t + half + 1)
                    s.activation(x[:, 4 * half:4 * half + 4, cols(t)],
                                 bank[2 * (t % 2) + half][:, 0:4 * ROWS[t]].rearrange("p (k n) -> p k n", k=4),
                                 ACT.Copy).then_inc(xT_evac, 1)
            squares(0)
            for l in range(DEPTH):
                def evac(c, t):
                    act.wait_ge(proj_done, NT * (4 * l + c) + t + 1)
                    rows, src = ROWS[t], bank[t]
                    if c == KVQI:
                        dst = z[0:rows, t, 0:CW]
                    elif c == GV:
                        dst = gvn[0:rows, t, :]
                    elif c == UU:
                        dst = ug[0:rows, t, :]
                    if c == QQ:
                        s.activation(q[0:rows, t, :].rearrange("p (b j d) -> p j b d", j=2, d=HD),
                                     src[0:rows, :].rearrange("p (j b d) -> p j b d", j=2, d=HD),
                                     ACT.Copy, scale=r[0:rows, t:t + 1]).then_inc(proj_evac, 1)
                    else:
                        s.activation(dst, src[0:rows, :], ACT.Copy if c == KVQI else ACT.Gelu_apprx_tanh,
                                     scale=r[0:rows, t:t + 1]).then_inc(proj_evac, 1)

                def gating_square(t):
                    act.wait_ge(proj_evac, NT * (4 * l + GV) + t + 1)
                    if t >= 2:
                        act.wait_ge(gv_sq, NT * l + t - 1)
                    s.activation(pr[0:ROWS[t], t % 2, :], gvn[0:ROWS[t], t, :], ACT.Square,
                                 accum_out=ssv[0:ROWS[t], t:t + 1]).then_inc(gv_sq, 1)

                act.wait_ge(ms_ready, l + 1)
                s.activation(r[:, :], r[:, :], ACT.Sqrt).then_inc(root_ready, 1)
                act.wait_ge(r_ready, l + 1)
                for t in range(NT):
                    evac(KVQI, t)
                for t in range(NT):
                    evac(QQ, t)
                for c in (GV, UU):
                    for half in range(2):
                        for t in range(NT):
                            if half == 1:
                                evac(c, t)
                                if c == GV and t:
                                    gating_square(t - 1)
                            if c == UU and half == 0 and t == 0:
                                gating_square(NT - 1)
                            for i in index_after(c, half, t):
                                ti, hh = INDEX[i]
                                act.wait_ge(idx_done, NX * l + i + 1)
                                if i >= 3:
                                    act.wait_ge(idx_acc, NX * l + i - 2)
                                s.activation(rl[0:ROWS[ti], i % 3, 0:KEYS[ti]], bank[5 + i % 2][0:ROWS[ti], 0:KEYS[ti]],
                                             ACT.Relu).then_inc(idx_relu, 1)

                def exp(i):
                    t, hh = ITEMS[i]
                    act.wait_ge(masked, NI * l + i + 1)
                    if i >= 2:
                        act.wait_ge(pT_done, NI * l + i - 1)
                    s.activation(pr[0:ROWS[t], i % 2, 0:KEYS[t]], L[0:ROWS[t], i % 3, 0:KEYS[t]], ACT.Exp,
                                 scale=-1.0, bias=nmax[0:ROWS[t], i:i + 1],
                                 accum_out=rsum[0:ROWS[t], i:i + 1]).then_inc(exp_done, 1)

                def pT_copy(i):
                    t, hh = ITEMS[i]
                    act.wait_ge(pT_done, NI * l + i + 1)
                    if i >= 2:
                        act.wait_ge(o_item, NI * l + i - 1)
                    n = -(-KEYS[t] // P) * ROWS[t]
                    if t == SMP:
                        s.activation(pT[:, i % 2, 0:DEC], bank[2 + i % 2][:, 0:DEC], ACT.Copy)
                        s.activation(pT[0:DEC, i % 2, DEC:2 * DEC], bank[2 + i % 2][0:DEC, DEC:2 * DEC],
                                     ACT.Copy).then_inc(pT_evac, 1)
                    else:
                        s.activation(pT[:, i % 2, 0:n], bank[2 + i % 2][:, 0:n], ACT.Copy).then_inc(pT_evac, 1)

                def mt_copy(a, part):
                    t = TILE_ORDER[a]
                    act.wait_ge(mt_done, 2 * NT * l + 2 * a + part + 1)
                    k0 = 0 if part == 0 else KT // 2
                    s.activation(mixT[:, k0:k0 + 4, cols(t)], bank[7][:, 0:4 * ROWS[t]].rearrange("p (k n) -> p k n", k=4),
                                 ACT.Copy).then_inc(mt_evac, 1)

                act.wait_ge(mv_ready, l + 1)
                s.activation(rv[:, :], rv[:, :], ACT.Sqrt).then_inc(root_ready, 1)
                exp(0)
                for i in range(NI):
                    if i + 1 < NI:
                        exp(i + 1)
                    pT_copy(i)
                    if i % NH == 4 and i > NH:
                        mt_copy(i // NH - 1, 0)
                        mt_copy(i // NH - 1, 1)
                mt_copy(NT - 1, 0)
                mt_copy(NT - 1, 1)
                squares(KT * (2 * l + 1))
                for f in range(FT):
                    n = FT * l + f
                    act.wait_ge(f1_done, n + 1)
                    if f >= 2:
                        act.wait_ge(h_ready, n - 1)
                    b = 2 * (f % 4)
                    for half in range(2):
                        last = s.activation(rl2[:, f % 2, half * HALF:(half + 1) * HALF], bank[b + half][:, 0:HALF], ACT.Relu)
                    last.then_inc(f1_relu, 1)
                squares(KT * (2 * l + 2))
            act.wait_ge(ms_ready, DEPTH + 1)
            s.activation(r[:, :], r[:, :], ACT.Sqrt).then_inc(root_ready, 1)
            act.wait_ge(r_ready, DEPTH + 1)
            for t in range(NT):
                for half in range(2):
                    n = 2 * t + half
                    act.wait_ge(fin_done, n + 1)
                    s.activation(out_b[0:ROWS[t], t, half * 512:(half + 1) * 512], bank[n % 4][0:ROWS[t], :], ACT.Copy,
                                 scale=r[0:ROWS[t], t:t + 1]).then_inc(fin_evac, 1)

        @block.vector
        def _(dve):
            v = nc.vector
            count = [0]

            def link(ins):
                count[0] += 1
                ins.then_inc(dve_step, 1)
                dve.wait_ge(dve_step, count[0])

            def feed(j, base, stage):
                dve.wait_ge(x_ready, base + j + 1)
                v.tensor_scalar(xg[:, j, :], x[:, j, :], gcol[:, stage_col(stage) + j:stage_col(stage) + j + 1], None, ALU.mult)\
                    .then_inc(xg_ready, 1)

            def stage_col(stage):
                return 2 * DEPTH * KT if stage == 2 * DEPTH else (stage % 2) * DEPTH * KT + stage // 2 * KT

            def row_mean(n):
                dve.wait_ge(ss_done, n + 1)
                link(v.tensor_scalar(ms[:, :], bank[5][:, 0:NT], 1.0 / D, EPS, ALU.mult, ALU.add))
                v.reciprocal(r[:, :], ms[:, :]).then_inc(ms_ready, 1)

            dve.wait_ge(gT_done, 1)
            v.tensor_copy(gcol[:, :], bank[7][:, 0:7 * KT]).then_inc(g_ready, 1)
            dve.wait_ge(g_ready, 1)
            dve.wait_ge(xT_evac, 2 * NT)
            for j in range(KT):
                v.tensor_scalar(xg[:, j, :], x[:, j, :], gcol[:, j:j + 1], None, ALU.mult).then_inc(xg_ready, 1)
            v.memset(yb[:, 0, 0:8], 0.0).then_inc(x_ready, KT)
            for l in range(DEPTH):
                row_mean(l)
                dve.wait_ge(r_ready, l + 1)
                dve.wait_ge(small_done, l + 1)
                v.tensor_tensor(z[:, 0:NPT, CW:ZW], bank[5][:, 0:NPT * NSM].rearrange("p (t n) -> p t n", t=NPT),
                                r[:, 0:NPT].rearrange("p (t o) -> p t o", o=1).broadcast_to([P, NPT, NSM]), ALU.mult)
                v.tensor_scalar(z[0:DEC, SMP, CW:ZW], bank[5][0:DEC, NPT * NSM:NT * NSM], r[0:DEC, SMP:SMP + 1], None,
                                ALU.mult).then_inc(small_evac, 1)
                dst = [kT[:, :], kTs[:, :], kiT[:, :], kiTs[:, :]]
                width = [SEQ, PAST + DEC, SEQ, PAST + DEC]
                wT_n = [0]

                def tr_copy(n):
                    dve.wait_ge(tr_done, (NTR + 2) * l + n + 1)
                    if n < 2:
                        out, src = w_spT[:, 4 * n:4 * n + 4, :], bank[7][:, :].rearrange("p (g n) -> p g n", g=4)
                    elif n < 6:
                        out, src = dst[n - 2], bank[7][:, 0:width[n - 2]]
                    elif n < 8:
                        out, src = qiT[:, n - 6, P:TOK], bank[7][:, 0:TOK - P]
                    elif n < 12:
                        out, src = qT[:, n - 8, 0:SEQ], bank[7][:, :]
                    else:
                        out, src = qT[:, :, SEQ:TOK], bank[7][:, 0:4 * DEC].rearrange("p (b n) -> p b n", b=4)
                    v.tensor_copy(out, src).then_inc(tr_evac, 1)

                for n in range(8):
                    tr_copy(n)
                    if n == 1:
                        dve.wait_ge(tr_evac, (NTR + 2) * l + 2)
                        v.memset(w_spT[CHUNK:P, :, 0:CHUNK], 0.0).then_inc(spT_ready, 1)

                def index_add(i):
                    t, hh = INDEX[i]
                    S, rows = KEYS[t], ROWS[t]
                    dve.wait_ge(idx_relu, NX * l + i + 1)
                    w = wi[0:rows, t, hh:hh + 1]
                    if hh == 0:
                        v.tensor_scalar(score[t][0:rows, :], rl[0:rows, i % 3, 0:S], w, None, ALU.mult).then_inc(idx_acc, 1)
                    else:
                        dve.wait_ge(idx_acc, NX * l + i)
                        v.scalar_tensor_tensor(score[t][0:rows, :], rl[0:rows, i % 3, 0:S], w, score[t][0:rows, :],
                                               ALU.mult, ALU.add).then_inc(idx_acc, 1)

                def topk_round(t, n):
                    rows = ROWS[t]
                    link(v.max(m8[0:rows, 1, :], score[t][0:rows, :]))
                    link(v.match_replace(score[t][0:rows, :], m8[0:rows, 1, :], score[t][0:rows, :], TAKEN))

                def mask_of(t):
                    rows = ROWS[t]
                    link(v.tensor_scalar(score[t][0:rows, :], score[t][0:rows, :], SPLIT, OFF, ALU.is_gt, ALU.mult))

                def rounds(t):
                    return (TOP_S if t == SMP else TOP_P) // 8

                def masked_logits(i):
                    t, hh = ITEMS[i]
                    rows, S = ROWS[t], KEYS[t]
                    dve.wait_ge(qk_done, NI * l + i + 1)
                    if i >= 3:
                        dve.wait_ge(exp_done, NI * l + i - 2)
                    mk = mask0[0:rows, :] if t == 0 else score[t][0:rows, :]
                    v.tensor_tensor_reduce(out=L[0:rows, i % 3, 0:S], in0=bank[i % 2][0:rows, 0:S], in1=mk,
                                           scale=-SCALE, scalar=3e38, op0=ALU.add, op1=ALU.min,
                                           accum_out=nmax[0:rows, i:i + 1]).then_inc(masked, 1)

                def gv_norm(t):
                    v.scalar_tensor_tensor(gvn[0:ROWS[t], t, :], gvn[0:ROWS[t], t, :], rv[0:ROWS[t], t:t + 1],
                                           gate_bc[0:ROWS[t], :], ALU.mult, ALU.mult).then_inc(gvn_ready, 1)

                def mix_copy(a):
                    t = TILE_ORDER[a]
                    dve.wait_ge(mix_done, NT * l + a + 1)
                    if a >= 2:
                        dve.wait_ge(bm_ready, NT * l + a - 1)
                    c0 = (2 * DEPTH + 1) * KT + l * NG
                    v.tensor_tensor(mb[0:ROWS[t], a % 2, :].rearrange("p (g c) -> p g c", g=NG),
                                    bank[6][0:ROWS[t], :].rearrange("p (g c) -> p g c", g=NG),
                                    gcol[0:ROWS[t], c0:c0 + NG].rearrange("p (g o) -> p g o", o=1)
                                    .broadcast_to([ROWS[t], NG, CPG]), ALU.add).then_inc(mix_evac, 1)

                def o_copy(a):
                    t = TILE_ORDER[a]
                    rows = ROWS[t]
                    dve.wait_ge(o_item, NI * l + NH * (a + 1))
                    link(v.reciprocal(rinv[0:rows, NH * a:NH * (a + 1)], rsum[0:rows, NH * a:NH * (a + 1)]))
                    v.tensor_tensor(o[0:rows, a % 2, :].rearrange("p (h d) -> p h d", h=NH),
                                    bank[4 + a % 2][0:rows, :].rearrange("p (h d) -> p h d", h=NH),
                                    rinv[0:rows, NH * a:NH * (a + 1)].rearrange("p (h o) -> p h o", o=1)
                                    .broadcast_to([rows, NH, HD]), ALU.mult).then_inc(o_ready, 1)

                for i in range(NX):
                    index_add(i)
                    if i % NIH == NIH - 1:
                        t = INDEX[i][0]
                        dve.wait_ge(idx_acc, NX * l + i + 1)
                        if t != SMP:
                            link(v.memset(score[t][0:CHUNK, KEYS[t] - CHUNK:KEYS[t]], NEG))
                    if i == NX // 2:
                        for n in range(8, 13):
                            tr_copy(n)
                for t in (SMP, 1):
                    for n in range(rounds(t)):
                        topk_round(t, n)
                    mask_of(t)
                dve.wait_ge(gv_sq, NT * (l + 1))
                link(v.tensor_scalar(mv[:, :], ssv[:, :], 1.0 / DB, EPS, ALU.mult, ALU.add))
                v.reciprocal(rv[:, :], mv[:, :]).then_inc(mv_ready, 1)
                dve.wait_ge(rv_ready, l + 1)
                for t in range(NT):
                    gv_norm(t)
                for i in range(NI):
                    a = i // NH
                    if i % NH == 0:
                        mix_copy(a)
                    if a < 2:
                        topk_round(2, i)
                        if i == 2 * NH - 1:
                            mask_of(2)
                    elif a < 4:
                        topk_round(3, i - 2 * NH)
                        if i == 4 * NH - 1:
                            mask_of(3)
                    masked_logits(i)
                    if i % NH == 3 and a:
                        o_copy(a - 1)
                o_copy(NT - 1)

                for j in range(KT):
                    dve.wait_ge(out_done, KT * l + j + 1)
                    for half in range(2):
                        last = v.tensor_tensor(x[:, j, half * HALF:(half + 1) * HALF], x[:, j, half * HALF:(half + 1) * HALF],
                                               bank[2 * (j % 2) + half][:, 0:HALF], ALU.add)
                    last.then_inc(x_ready, 1)
                    feed(j, KT * (2 * l + 1), 2 * l + 1)
                dve.wait_ge(ssb_done, l + 1)
                for half in range(2):
                    last = v.tensor_scalar(r2b[:, half * HALF:(half + 1) * HALF], bank[6 + half][:, 0:HALF], 1.0 / D, EPS,
                                           ALU.mult, ALU.add)
                last.then_inc(ssb_read, 1)
                dve.wait_ge(ssb_read, l + 1)
                link(v.reciprocal(r2b[:, :], r2b[:, :]))
                dve.wait_ge(kv_out, 16 * KV_OUTS * (l + 1))
                for f in range(FT):
                    dve.wait_ge(f1_relu, FT * l + f + 1)
                    v.tensor_tensor(h[:, f, :], rl2[:, f % 2, :], rl2[:, f % 2, :], ALU.mult).then_inc(h_ready, 1)
                for j in range(KT):
                    dve.wait_ge(f2_done, KT * l + j + 1)
                    b = 4 * (j // 2 % 2) + 2 * (j % 2)
                    for half in range(2):
                        last = v.tensor_tensor(yb[:, j % 2, half * HALF:(half + 1) * HALF],
                                               r2b[:, half * HALF:(half + 1) * HALF], bank[b + half][:, 0:HALF], ALU.mult)
                    last.then_inc(y_ready, 1)
                    dve.wait_ge(y_ready, KT * l + j + 1)
                    v.tensor_tensor(x[:, j, :], x[:, j, :], yb[:, j % 2, :], ALU.add).then_inc(x_ready, 1)
                    feed(j, KT * (2 * l + 2), 2 * l + 2)
            row_mean(DEPTH)

        @block.tensor
        def _(pe):
            mm = nc.tensor.matmul
            tp = nc.tensor.transpose

            def row_sums(n):
                pe.wait_ge(ss_added, KT * (2 * n + 1))
                for t in range(NT):
                    last = mm(bank[5][:, t:t + 1], ssacc[:, t * P:(t + 1) * P], ones[:, 0:1], start=True, stop=True)
                last.then_inc(ss_done, 1)

            pe.wait_ge(const_made, 5)
            pe.wait_ge(const_in, 16 * 5)
            tp(bank[7][:, 0:7 * KT], grow[:, :], ident[0:7 * KT, 0:7 * KT]).then_inc(gT_done, 1)
            pe.wait_ge(x_loaded, 32)
            for t in range(NT):
                for half in range(2):
                    if t >= 2:
                        pe.wait_ge(xT_evac, 2 * t + half - 3)
                    for k in range(4):
                        last = tp(bank[2 * (t % 2) + half][:, k * ROWS[t]:(k + 1) * ROWS[t]],
                                  x_in[0:ROWS[t], t, (4 * half + k) * P:(4 * half + k + 1) * P],
                                  ident[0:ROWS[t], 0:ROWS[t]])
                    last.then_inc(xT_done, 1)

            for l in range(DEPTH):
                def slot(n):
                    pe.wait_ge(w_ready[n % NSLOT], 16 * (l * (SLOTS // NSLOT) + n // NSLOT + 1))

                def group(c, half, t):
                    if half == 0:
                        if c:
                            pe.wait_ge(proj_evac, NT * (4 * l + c - 1) + t + 1)
                    w = ring[:, (2 * c + half) % NSLOT, :].rearrange("p (k n) -> p k n", k=KT // 2)
                    for k in range(4):
                        kk = 4 * half + k
                        last = mm(bank[t][0:ROWS[t], :], xg[:, kk, cols(t)], w[:, k, :], start=kk == 0, stop=kk == KT - 1)
                    if half:
                        last.then_inc(proj_done, 1)
                    elif t == NT - 1:
                        last.then_inc(half_done, 1)

                def chunk_half(c, half):
                    slot(2 * c + half)
                    for t in range(NT):
                        group(c, half, t)
                        for i in index_after(c, half, t):
                            index(i)

                def index(i):
                    t, hh = INDEX[i]
                    if i == 0:
                        pe.wait_ge(tr_evac, (NTR + 2) * l + 8)
                    if i >= 2:
                        pe.wait_ge(idx_relu, NX * l + i - 1)
                    b, rows = 32 * (hh % 4), ROWS[t]
                    keys = kiTs if t == SMP else kiT
                    mm(bank[5 + i % 2][0:rows, 0:KEYS[t]], qiT[b:b + ID, hh // 4, cols(t)], keys[b:b + ID, 0:KEYS[t]],
                       start=True, stop=True).then_inc(idx_done, 1)

                tr = [0]

                def tr_group(parts):
                    n = (NTR + 2) * l + tr[0]
                    if n:
                        pe.wait_ge(tr_evac, n)
                    c0 = 0
                    for src in parts:
                        rows = src.shape[0]
                        last = tp(bank[7][:, c0:c0 + rows], src, ident[0:rows, 0:rows])
                        c0 += rows
                    last.then_inc(tr_done, 1)
                    tr[0] += 1

                pe.wait_ge(xg_ready, KT * (2 * l + 1))
                chunk_half(KVQI, 0)
                row_sums(l)
                chunk_half(KVQI, 1)
                pe.wait_ge(ws_in, 16 * (l + 1))
                pe.wait_ge(ms_ready, l + 1)
                for t in range(NT):
                    for k in range(KT):
                        last = mm(bank[5][0:ROWS[t], t * NSM:(t + 1) * NSM], xg[:, k, cols(t)], w_small[:, k, :],
                                  start=k == 0, stop=k == KT - 1)
                last.then_inc(small_done, 1)
                chunk_half(QQ, 0)
                pe.wait_ge(small_in, 16 * 5 * (l + 1))
                for n in range(2):
                    tr_group([w_sp[:, 4 * n + g, :] for g in range(4)])
                pe.wait_ge(roped, l + 1)
                zz = lambda t, a, b: z[0:ROWS[t], t, a:b]
                tr_group([zz(t, Z_K, Z_K + DKV) for t in range(NPT)])
                tr_group([cache_k[:, :], zz(SMP, Z_K, Z_K + DKV)])
                tr_group([ki4[:, t, :] for t in range(NPT)])
                tr_group([cache_ki4[:, :, :].rearrange("p a d -> p (a d)"), ki4[0:DEC, SMP, :]])
                for b in range(2):
                    tr_group([zz(t, Z_QI + b * P, Z_QI + (b + 1) * P) for t in list(range(1, NPT)) + [SMP]])
                chunk_half(QQ, 1)
                chunk_half(GV, 0)
                chunk_half(GV, 1)
                pe.wait_ge(q_roped, l + 1)
                for b in range(4):
                    tr_group([q[:, t, b * P:(b + 1) * P] for t in range(NPT)])
                tr_group([q[0:DEC, SMP, b * P:(b + 1) * P] for b in range(4)])
                chunk_half(UU, 0)
                chunk_half(UU, 1)

                def scores_of(i):
                    t, hh = ITEMS[i]
                    if i == 0:
                        pe.wait_ge(tr_evac, (NTR + 2) * (l + 1))
                        pe.wait_ge(proj_evac, 4 * NT * (l + 1))
                        pe.wait_ge(idx_relu, NX * (l + 1))
                    if i >= 2:
                        pe.wait_ge(masked, NI * l + i - 1)
                    b = HD * (hh // 4)
                    keys = kTs if t == SMP else kT
                    mm(bank[i % 2][0:ROWS[t], 0:KEYS[t]], qT[b:b + HD, hh % 4, cols(t)], keys[b:b + HD, 0:KEYS[t]],
                       start=True, stop=True).then_inc(qk_done, 1)

                def p_transpose(i):
                    t, hh = ITEMS[i]
                    pe.wait_ge(exp_done, NI * l + i + 1)
                    if i >= 2:
                        pe.wait_ge(pT_evac, NI * l + i - 1)
                    for s0 in range(0, KEYS[t], P):
                        n = min(P, KEYS[t] - s0)
                        c0 = s0 // P * ROWS[t]
                        last = tp(bank[2 + i % 2][0:n, c0:c0 + ROWS[t]], pr[0:ROWS[t], i % 2, s0:s0 + n],
                                  ident[0:ROWS[t], 0:ROWS[t]])
                    last.then_inc(pT_done, 1)

                def weighted(i):
                    t, hh = ITEMS[i]
                    a = i // NH
                    pe.wait_ge(pT_evac, NI * l + i + 1)
                    if hh == 0 and a >= 2:
                        pe.wait_ge(o_ready, NT * l + a - 1)
                    nb = -(-KEYS[t] // P)
                    g0 = Z_V + HD * (hh // 4)
                    for s in range(nb):
                        n = min(P, KEYS[t] - s * P)
                        if t == SMP:
                            vals = cache_v[:, HD * (hh // 4):HD * (hh // 4) + HD] if s == 0 else z[0:DEC, SMP, g0:g0 + HD]
                        else:
                            vals = z[:, s, g0:g0 + HD]
                        last = mm(bank[4 + a % 2][0:ROWS[t], hh * HD:(hh + 1) * HD],
                                  pT[0:n, i % 2, s * ROWS[t]:(s + 1) * ROWS[t]], vals, start=s == 0, stop=s == nb - 1)
                    last.then_inc(o_item, 1)

                def spatial(a):
                    t = TILE_ORDER[a]
                    pe.wait_ge(spT_ready, l + 1)
                    pe.wait_ge(gvn_ready, NT * (l + 1))
                    if a:
                        pe.wait_ge(mix_evac, NT * l + a)
                    rows = ROWS[t]
                    for g in range(NG):
                        last = mm(bank[6][0:rows, g * CPG:(g + 1) * CPG], w_spT[0:rows, g, 0:rows],
                                  gvn[0:rows, t, g * CPG:(g + 1) * CPG], start=True, stop=True)
                    last.then_inc(mix_done, 1)

                def mt_group(a, part):
                    t = TILE_ORDER[a]
                    n = 2 * NT * l + 2 * a + part
                    if n:
                        pe.wait_ge(mt_evac, n)
                    pe.wait_ge(o_ready if part == 0 else bm_ready, NT * l + a + 1)
                    src = o[0:ROWS[t], a % 2, :] if part == 0 else ug[0:ROWS[t], t, :]
                    for k in range(4):
                        last = tp(bank[7][:, k * ROWS[t]:(k + 1) * ROWS[t]], src[:, k * P:(k + 1) * P],
                                  ident[0:ROWS[t], 0:ROWS[t]])
                    last.then_inc(mt_done, 1)

                scores_of(0)
                scores_of(1)
                for i in range(NI):
                    if i % NH == 0:
                        spatial(i // NH)
                    if i + 2 < NI:
                        scores_of(i + 2)
                    p_transpose(i)
                    if i:
                        weighted(i - 1)
                    if i % NH == 4 and i > NH:
                        mt_group(i // NH - 1, 0)
                        mt_group(i // NH - 1, 1)
                weighted(NI - 1)
                mt_group(NT - 1, 0)
                mt_group(NT - 1, 1)
                mm(bank[6][0:2, 0:2], ones[:, 0:2], ones[:, 0:2], start=True, stop=True).then_inc(layer_buf_free, 1)

                pe.wait_ge(mt_evac, 2 * NT * (l + 1))
                for p_ in range(NPAIR):
                    slot(S_OUT + p_)
                    w = ring[:, (S_OUT + p_) % NSLOT, :].rearrange("p (k n) -> p k n", k=KT)
                    for jj in range(2):
                        j = 2 * p_ + jj
                        if j >= 2:
                            pe.wait_ge(x_ready, KT * (2 * l + 1) + j - 1)
                        for k in range(KT):
                            for half in range(2):
                                last = mm(bank[2 * (j % 2) + half][:, 0:HALF], w[:, k, jj * P:(jj + 1) * P],
                                          mixT[:, k, half * HALF:(half + 1) * HALF], start=k == 0, stop=k == KT - 1)
                        last.then_inc(out_done, 1)
                pe.wait_ge(xg_ready, KT * (2 * l + 2))
                for f in range(FT):
                    n = S_F1 + f // 2
                    if f % 2 == 0:
                        slot(n)
                    w = ring[:, n % NSLOT, :].rearrange("p (k n) -> p k n", k=KT)
                    if f == 3:
                        pe.wait_ge(ssb_read, l + 1)
                    if f >= 4:
                        pe.wait_ge(f1_relu, FT * l + f - 3)
                    for k in range(KT):
                        for half in range(2):
                            last = mm(bank[2 * (f % 4) + half][:, 0:HALF], w[:, k, f % 2 * P:(f % 2 + 1) * P],
                                      xg[:, k, half * HALF:(half + 1) * HALF], start=k == 0, stop=k == KT - 1)
                    last.then_inc(f1_done, 1)
                    if f == 1:
                        pe.wait_ge(ss_added, KT * (2 * l + 2))
                        for half in range(2):
                            last = mm(bank[6 + half][:, 0:HALF], ones[:, :], ssacc[:, half * HALF:(half + 1) * HALF],
                                      start=True, stop=True)
                        last.then_inc(ssb_done, 1)
                for jp in range(NPAIR):
                    for m in range(NSLOT):
                        n = S_F2 + NSLOT * jp + m
                        slot(n)
                        w = ring[:, n % NSLOT, :].rearrange("p (k n) -> p k n", k=KT)
                        if jp == 0 and m == 0:
                            pe.wait_ge(f1_relu, FT * (l + 1))
                        if m == 0 and jp >= 2:
                            pe.wait_ge(y_ready, KT * l + 2 * jp - 2)
                        pe.wait_ge(h_ready, FT * l + KT * (m + 1))
                        for jj in range(2):
                            for k in range(KT):
                                for half in range(2):
                                    last = mm(bank[4 * (jp % 2) + 2 * jj + half][:, 0:HALF], w[:, k, jj * P:(jj + 1) * P],
                                              h[:, KT * m + k, half * HALF:(half + 1) * HALF],
                                              start=m == 0 and k == 0, stop=m == NSLOT - 1 and k == KT - 1)
                            if m == NSLOT - 1:
                                last.then_inc(f2_done, 1)
                        if m < NSLOT - 1:
                            last.then_inc(half_done, 1)
            pe.wait_ge(xg_ready, KT * (2 * DEPTH + 1))
            row_sums(DEPTH)
            for t in range(NT):
                for half in range(2):
                    n = 2 * t + half
                    if n >= 4:
                        pe.wait_ge(fin_evac, n - 3)
                    for k in range(4):
                        last = tp(bank[n % 4][0:ROWS[t], k * P:(k + 1) * P], xg[:, 4 * half + k, cols(t)], ident[:, :])
                    last.then_inc(fin_done, 1)


_INS = ['x_prompt', 'x_sample', 'cache_k', 'cache_v', 'cache_kidx', 'norm_mix', 'w_in', 'gate_norm', 'w_spatial',
        'b_spatial', 'w_out', 'norm_ffn', 'w_ff1', 'w_ff2', 'norm_final']


def kernel(**inputs):
    import numpy as np
    import concourse.bacc as bacc
    from concourse import mybir
    from concourse.bass_utils import run_bass_kernel_spmd

    nc = bacc.Bacc("TRN2", target_bir_lowering=False, num_devices=1)
    arrays = {n: np.ascontiguousarray(inputs[n]) for n in _INS}
    L, B, past, nkv, hd = arrays['cache_k'].shape
    seq, d = arrays['x_prompt'].shape[1:]
    dec = arrays['x_sample'].shape[1]
    idd = arrays['cache_kidx'].shape[3]
    db = arrays['gate_norm'].shape[1]

    nt = seq // 128 + 1
    pos = np.arange(nt * 128).reshape(nt, 128).T.astype(np.float32)
    pos[:, nt - 1] = past + np.arange(128)
    parts = []
    for half in (hd // 8, idd // 8):
        inv = np.power(np.float32(500000.0), -np.arange(half, dtype=np.float32) * np.float32(2.0 / (2 * half)))
        ang = (pos[:, :, None] * inv.astype(np.float32)).astype(np.float32)
        c, s = np.cos(ang), np.sin(ang)
        parts += [c, c, -s, s]
    arrays['rope_table'] = np.concatenate(parts, -1).astype(np.float32)

    outs = {'y_prompt': (B, seq, d), 'y_sample': (B, dec, d), 'k_prompt': (L, B, seq, nkv, hd),
            'v_prompt': (L, B, seq, nkv, hd), 'kidx_prompt': (L, B, seq, idd), 'k_sample': (L, B, dec, nkv, hd),
            'v_sample': (L, B, dec, nkv, hd), 'kidx_sample': (L, B, dec, idd), 'gv_sample': (L, B, dec, db)}
    A = {n: nc.dram_tensor(f"in_{n}", a.shape, mybir.dt.from_np(a.dtype), kind="ExternalInput").ap()
         for n, a in arrays.items()}
    O = {n: nc.dram_tensor(f"out_{n}", s, mybir.dt.float32, kind="ExternalOutput").ap() for n, s in outs.items()}
    hybrid_encoder_program(nc, A, O)
    res = run_bass_kernel_spmd(nc, [{f"in_{n}": a for n, a in arrays.items()}], core_ids=[0])
    return tuple(res.results[0][f"out_{n}"] for n in outs)
```

```python
import concourse.bass as bass
from concourse import mybir
from contextlib import ExitStack


def hybrid_encoder_program(nc, A, O):
    F32 = mybir.dt.float32
    F32R = mybir.dt.float32r
    ALU = mybir.AluOpType
    ACT = mybir.ActivationFunctionType

    import numpy as np

    P = 128
    SEQ, D = A["x_prompt"].shape[1], A["x_prompt"].shape[2]
    DEC = A["x_sample"].shape[1]
    DEPTH, _, PAST, NKV, HD = A["cache_k"].shape
    ID = A["cache_kidx"].shape[3]
    N_IN = A["w_in"].shape[2]
    DB = A["gate_norm"].shape[1]
    NG = A["w_spatial"].shape[1]
    DFF = A["w_ff1"].shape[2]
    DA = D - DB
    NH = DA // HD
    NIH = 8
    CHUNK = 64
    KT = D // P
    FT = DFF // P
    CPG = DB // NG
    DKV = NKV * HD
    TOP_P, TOP_S = min(256, SEQ // 4), min(256, (PAST + DEC) // 4)
    EPS = 1e-6
    NPT = SEQ // P
    NT = NPT + 1
    SMP = NPT
    TOK = SEQ + DEC
    HALF = TOK // 2
    HALVES = [slice(0, HALF), slice(HALF, TOK)]
    ROWS = [P] * NPT + [DEC]
    KEYS = [P * (t + 1) for t in range(NPT)] + [PAST + DEC]
    RH, RI = HD // 8, ID // 8
    NEG, TAKEN, SPLIT, OFF = -2e38, -3e38, -2.5e38, -1e30
    SCALE = float(HD) ** -0.5

    C_Q, C_K = 0, DA
    C_SMALL = DA + 2 * DKV + NIH * ID
    NSM = ID + NIH
    C_U = C_SMALL + NSM
    C_GV = C_U + DB
    CW = 512
    CHUNKS = [C_K, C_Q, C_GV, C_U]
    KVQI, QQ, GV, UU = range(4)
    ZW = CW + NSM
    Z_K, Z_V, Z_QI, Z_KI, Z_WI = 0, DKV, 2 * DKV, CW, CW + ID

    NRAW, NSLOT = 2, 4
    SW = KT * P
    QUARTERS = SW // CW and D // (SW // CW * P)
    KQ = SW // CW
    GROUPS = FT // KT
    S_OUT = QUARTERS * len(CHUNKS)
    S_FFN = S_OUT + KT
    UNITS = KT + 2 * KT * GROUPS
    SLOTS = S_FFN + 2 * KT * GROUPS

    TILE_ORDER = [0, SMP] + list(range(1, NPT))
    ITEMS = [(t, h) for t in TILE_ORDER for h in range(NH)]
    NI = len(ITEMS)
    INDEX_TILES = [SMP] + list(range(1, NPT))
    INDEX = [(t, h) for t in INDEX_TILES for h in range(NIH)]
    NX = len(INDEX)

    def cols(t):
        return slice(t * P, t * P + ROWS[t])

    ctx = ExitStack()
    with ctx:
        def sb(name, shape, dt=F32):
            return ctx.enter_context(nc.sbuf_tensor(name, shape, dt))

        def sem(name):
            return ctx.enter_context(nc.semaphore(name))

        x = sb("x", [P, KT, TOK])
        ring_raw = sb("ring_raw", [P, NRAW, SW])
        ring_hi = sb("ring_hi", [P, NSLOT, SW], F32R)
        ring_lo = sb("ring_lo", [P, NSLOT, SW], F32R)
        w_small = sb("w_small", [P, KT, NSM])
        w_small_r = sb("w_small_r", [P, KT, 2, NSM], F32R)
        ident = sb("ident", [P, P])
        ones = sb("ones", [P, P])
        grow = sb("grow", [7 * KT, P])
        gcol = sb("gcol", [P, 7 * KT])
        rope_t = sb("rope_t", [P, NT, 4 * RH + 4 * RI])
        w_spT = sb("w_spT", [P, NG, P])
        gate_bc = sb("gate_bc", [P, DB])
        cache_k = sb("cache_k_t", [P, DKV])
        cache_v = sb("cache_v_t", [P, DKV])
        cache_ki = sb("cache_ki_t", [P, ID])
        cache_ki4 = sb("cache_ki4", [P, 4, ID])
        ssacc = sb("ssacc", [P, NT * P])
        ms = sb("ms", [P, NT])
        r = sb("r", [P, NT])
        ssv = sb("ssv", [P, NT])
        rv = sb("rv", [P, NT])
        mv = sb("mv", [P, NT])
        nw = sb("nw", [P, NT])
        wi = sb("wi", [P, NT, NIH])
        m8 = sb("m8", [P, 2, 8])
        mask0 = sb("mask0", [P, P])
        nmax = sb("nmax", [P, NI])
        rsum = sb("rsum", [P, NI])
        rinv = sb("rinv", [P, NI])
        z = sb("z", [P, NT, ZW])

        class Area:
            def __init__(self, name, size):
                self.all, self.used = sb(name, [P, size]), 0

            def take(self, *dims):
                n = int(np.prod(dims))
                v = self.all[:, self.used:self.used + n]
                self.used += n
                assert self.used <= self.all.shape[1], self.used
                if len(dims) == 1:
                    return v
                if len(dims) == 2:
                    return v.rearrange("p (a b) -> p a b", a=dims[0])
                return v.rearrange("p (a b c) -> p a b c", a=dims[0], b=dims[1])

        late = Area("late", 2 * NT * DB + SEQ + PAST + DEC + sum(KEYS[1:]) + 4 * TOK)
        ug, gvn = late.take(NT, DB), late.take(NT, DB)
        kT, kTs = late.take(SEQ), late.take(PAST + DEC)
        at = late.used
        score = {t: late.take(KEYS[t]) for t in INDEX_TILES}
        late.used = at
        w_sp = late.take(NG, P)
        late.used = at + sum(KEYS[1:])
        qT = late.take(4, TOK)
        ki4 = qT[:, :, :].rearrange("p a b -> p (a b)")[:, 0:NT * 4 * ID].rearrange("p (t n) -> p t n", t=NT)
        late.used = 0
        sq, rl2, yb, h32 = (late.take(2, TOK) for _ in range(4))
        r2b = late.take(TOK)
        late.used = 0
        x_in = late.take(NT, D)
        out_b = x_in

        with ExitStack() as area:
            def sb(name, shape, dt=F32):
                return area.enter_context(nc.sbuf_tensor(name, shape, dt))
            att = Area("att", 3 * SEQ + 4 * SEQ + 2 * DA + 2 * DB)
            L, pr, pT = att.take(3, SEQ), att.take(2, SEQ), att.take(2, SEQ)
            o, mb = att.take(2, DA), att.take(2, DB)

        def sb(name, shape, dt=F32):
            return ctx.enter_context(nc.sbuf_tensor(name, shape, dt))
        xh = sb("xh", [P, KT, TOK], F32R)
        xl = sb("xl", [P, KT, TOK], F32R)

        with ExitStack() as area:
            def sb(name, shape, dt=F32):
                return area.enter_context(nc.sbuf_tensor(name, shape, dt))
            early = Area("early", NT * DA + 2 * NT * NH * 2 * RH + 3 * SEQ)
            q = early.take(NT, DA)
            ra, rb = early.take(NT, NH * 2 * RH), early.take(NT, NH * 2 * RH)
            zs2 = early.all[:, 0:NT * NSM].rearrange("p (t n) -> p t n", t=NT)
            gsq = early.all[:, NT * DA:NT * DA + 2 * DB].rearrange("p (a b) -> p a b", a=2)
            rl = early.take(3, SEQ)
            qih, qil = sb("qih", [P, 2, TOK], F32R), sb("qil", [P, 2, TOK], F32R)
            kih, kil = sb("kih", [P, SEQ], F32R), sb("kil", [P, SEQ], F32R)
            kish, kisl = sb("kish", [P, PAST + DEC], F32R), sb("kisl", [P, PAST + DEC], F32R)

        def sb(name, shape, dt=F32):
            return ctx.enter_context(nc.sbuf_tensor(name, shape, dt))
        vh = sb("vh", [P, KT, TOK], F32R)
        vl = sb("vl", [P, KT, TOK], F32R)

        bank = [ctx.enter_context(nc.psum_tensor(f"bank{i}", [P, 512], F32)) for i in range(8)]

        w_ready = [sem(f"w_ready{s}") for s in range(NRAW)]
        hi_ready, lo_ready = sem("hi_ready"), sem("lo_ready")
        ws_hi, ws_split = sem("ws_hi"), sem("ws_split")
        xh_ready, vh_ready, vl_ready = sem("xh_ready"), sem("vh_ready"), sem("vl_ready")
        tr_hi, scaled = sem("tr_hi"), sem("scaled")
        quarter_done, unit_done, y_read = sem("quarter_done"), sem("unit_done"), sem("y_read")
        y_scaled = sem("y_scaled")
        const_in = sem("const_in")
        x_loaded = sem("x_loaded")
        small_in = sem("small_in")
        ws_in = sem("ws_in")
        const_made = sem("const_made")
        xT_done, xT_evac = sem("xT_done"), sem("xT_evac")
        gT_done, g_ready = sem("gT_done"), sem("g_ready")
        x_ready = sem("x_ready")
        sq_ready, ss_added = sem("sq_ready"), sem("ss_added")
        xl_ready = sem("xl_ready")
        ss_done, ms_ready, r_ready = sem("ss_done"), sem("ms_ready"), sem("r_ready")
        root_ready, mv_ready = sem("root_ready"), sem("mv_ready")
        proj_done, proj_evac = sem("proj_done"), sem("proj_evac")
        small_done, small_evac = sem("small_done"), sem("small_evac")
        roped, q_roped = sem("roped"), sem("q_roped")
        tr_done, tr_evac = sem("tr_done"), sem("tr_evac")
        idx_done, idx_relu, idx_acc = sem("idx_done"), sem("idx_relu"), sem("idx_acc")
        gv_sq, rv_ready, gvn_ready = sem("gv_sq"), sem("rv_ready"), sem("gvn_ready")
        mix_done, mix_evac, bm_ready = sem("mix_done"), sem("mix_evac"), sem("bm_ready")
        qk_done, masked, exp_done = sem("qk_done"), sem("masked"), sem("exp_done")
        pT_done, pT_evac = sem("pT_done"), sem("pT_evac")
        o_ready = sem("o_ready")
        mt_done, mt_evac = sem("mt_done"), sem("mt_evac")
        out_done = sem("out_done")
        o_item, spT_ready, y_ready = sem("o_item"), sem("spT_ready"), sem("y_ready")
        ssb_done, ssb_read = sem("ssb_done"), sem("ssb_read")
        f1_done, f1_relu, h_ready = sem("f1_done"), sem("f1_relu"), sem("h_ready")
        f2_done = sem("f2_done")
        fin_done, fin_evac = sem("fin_done"), sem("fin_evac")
        dve_step, pool_step = sem("dve_step"), sem("pool_step")
        kv_out = sem("kv_out")
        y_out = sem("y_out")

        block = ctx.enter_context(nc.Block())

        NTR1 = 6
        NTR = NTR1 + 5
        KV_OUTS = 7

        INDEX_AT = 7 * NT + 3

        def aux_after(n, t):
            g = n * NT + t
            out = []
            first = 5 * NT
            for k, at in enumerate([first, first + 2] + [6 * NT + 1 + i for i in range(4)] + [7 * NT, 7 * NT + 1]):
                if g == at:
                    out.append(("tr", k))
            if INDEX_AT <= g < INDEX_AT + NX:
                out.append(("index", g - INDEX_AT))
            if n == 12 and t < NTR + 2 - 8:
                out.append(("tr", 8 + t))
            return out

        def last_reader(n):
            l, n = n // SLOTS, n % SLOTS
            if n < S_OUT:
                c, k = divmod(n, QUARTERS)
                return (proj_done, NT * (4 * l + c + 1)) if k == QUARTERS - 1 else (quarter_done, 12 * l + 3 * c + k + 1)
            return unit_done, UNITS * l + n - S_OUT + 1

        def unit_read(u):
            l, u = u // UNITS, u % UNITS
            if u >= KT and (u - KT) % (2 * KT) < KT:
                f = (u - KT) // (2 * KT) * KT + (u - KT) % (2 * KT)
                return f1_relu, FT * l + f + 1
            j = u if u < KT else (u - KT) // (2 * KT) * KT + u % KT + KT
            return y_read, KT * (GROUPS + 1) * l + j + 1

        def raw_use(n):
            return 16 * (n // NRAW + 1)

        @block.sync
        def _(sp):
            sp.dma_start(x_in[:, 0:NPT, :], A["x_prompt"][0].rearrange("(t p) d -> p t d", p=P)).then_inc(x_loaded, 16)
            sp.dma_start(x_in[0:DEC, SMP, :], A["x_sample"][0]).then_inc(x_loaded, 16)
            row = 0
            for src in (A["norm_mix"], A["norm_ffn"], A["norm_final"], A["b_spatial"]):
                v = src.rearrange("l (k p) -> (l k) p", p=P) if len(src.shape) == 2 else (
                    src.rearrange("(k p) -> k p", p=P) if len(src.shape) == 1 else src.rearrange("l g p -> (l g) p"))
                sp.dma_start(grow[row:row + v.shape[0], :], v).then_inc(const_in, 16)
                row += v.shape[0]
            sp.dma_start(rope_t[:, :, :], A["rope_table"]).then_inc(const_in, 16)
            for l in range(DEPTH):
                n = [SLOTS * l]

                def load(src, runs):
                    if n[0] >= NRAW:
                        sp.wait_ge(lo_ready, n[0] - NRAW + 1)
                    sp.dma_start(ring_raw[:, n[0] % NRAW, :].rearrange("p (k n) -> p k n", k=runs), src)\
                        .then_inc(w_ready[n[0] % NRAW], 16)
                    n[0] += 1

                if l:
                    sp.wait_ge(unit_done, UNITS * (l - 1) + 1)
                sp.dma_start(w_small[:, :, :], A["w_in"][l, :, C_SMALL:C_SMALL + NSM]
                             .rearrange("(k p) n -> p k n", p=P)).then_inc(ws_in, 16)
                for c, c0 in enumerate(CHUNKS):
                    for k in range(QUARTERS):
                        load(A["w_in"][l, k * KQ * P:(k + 1) * KQ * P, c0:c0 + CW]
                             .rearrange("(k p) n -> p k n", p=P), KQ)
                    if c == 0:
                        sp.dma_start(cache_k[:, :], A["cache_k"][l, 0].rearrange("s h d -> s (h d)")).then_inc(small_in, 16)
                        sp.dma_start(cache_v[:, :], A["cache_v"][l, 0].rearrange("s h d -> s (h d)")).then_inc(small_in, 16)
                        sp.dma_start(cache_ki[:, :], A["cache_kidx"][l, 0]).then_inc(small_in, 16)
                        sp.dma_start(w_sp[:, :, :], A["w_spatial"][l].rearrange("g i j -> i g j")).then_inc(small_in, 16)
                        sp.dma_start(gate_bc[:, :], A["gate_norm"][l:l + 1, :].broadcast_to([P, DB])).then_inc(small_in, 16)
                for j in range(KT):
                    load(A["w_out"][l, :, j * P:(j + 1) * P].rearrange("(k p) n -> p k n", p=P), KT)
                    if j == 5:
                        sp.wait_ge(roped, l + 1)
                        zp = z[:, 0:NPT, :]
                        zs = z[0:DEC, SMP, :]
                        sp.dma_start(O["k_prompt"][l, 0].rearrange("(t p) h d -> p t (h d)", p=P), zp[:, :, Z_K:Z_K + DKV]).then_inc(kv_out, 16)
                        sp.dma_start(O["v_prompt"][l, 0].rearrange("(t p) h d -> p t (h d)", p=P), zp[:, :, Z_V:Z_V + DKV]).then_inc(kv_out, 16)
                        sp.dma_start(O["kidx_prompt"][l, 0].rearrange("(t p) d -> p t d", p=P), zp[:, :, Z_KI:Z_KI + ID]).then_inc(kv_out, 16)
                        sp.dma_start(O["k_sample"][l, 0].rearrange("p h d -> p (h d)"), zs[:, Z_K:Z_K + DKV]).then_inc(kv_out, 16)
                        sp.dma_start(O["v_sample"][l, 0].rearrange("p h d -> p (h d)"), zs[:, Z_V:Z_V + DKV]).then_inc(kv_out, 16)
                        sp.dma_start(O["kidx_sample"][l, 0], zs[:, Z_KI:Z_KI + ID]).then_inc(kv_out, 16)
                        sp.wait_ge(gvn_ready, NT * l + NT)
                        sp.dma_start(O["gv_sample"][l, 0], gvn[0:DEC, SMP, :]).then_inc(kv_out, 16)
                for g in range(GROUPS):
                    for f in range(KT * g, KT * (g + 1)):
                        load(A["w_ff1"][l, :, f * P:(f + 1) * P].rearrange("(k p) n -> p k n", p=P), KT)
                    for j in range(KT):
                        load(A["w_ff2"][l, g * D:(g + 1) * D, j * P:(j + 1) * P].rearrange("(k p) n -> p k n", p=P), KT)
            for t in range(NT):
                sp.wait_ge(fin_evac, 2 * t + 2)
                dst = O["y_prompt"][0, t * P:(t + 1) * P, :] if t < NPT else O["y_sample"][0]
                sp.dma_start(dst, out_b[0:ROWS[t], t, :]).then_inc(y_out, 16)
            sp.wait_ge(y_out, 16 * NT)
            sp.wait_ge(kv_out, 16 * KV_OUTS * DEPTH)

        def gain(stage, j):
            c = 2 * DEPTH * KT if stage == 2 * DEPTH else (stage % 2) * DEPTH * KT + stage // 2 * KT
            return gcol[:, c + j:c + j + 1]

        index_parts = [(kih[:, :], kil[:, :], SEQ), (kish[:, :], kisl[:, :], PAST + DEC),
                       (qih[:, 0, P:TOK], qil[:, 0, P:TOK], TOK - P), (qih[:, 1, P:TOK], qil[:, 1, P:TOK], TOK - P)]

        @block.gpsimd
        def _(pool):
            count = [0]

            def link(ins):
                count[0] += 1
                ins.then_inc(pool_step, 1)
                pool.wait_ge(pool_step, count[0])

            g = nc.gpsimd
            link(g.memset(ident[:, :], 0.0))
            g.affine_select(out=ident[:, :], in_=ident[:, :], compare_op=ALU.not_equal, fill=1.0, base=0,
                            pattern=[[-1, P]], channel_multiplier=1).then_inc(const_made, 1)
            g.memset(ones[:, :], 1.0).then_inc(const_made, 1)
            g.memset(ssacc[:, TOK:NT * P], 0.0).then_inc(const_made, 1)
            g.memset(ssv[:, :], 1.0).then_inc(const_made, 1)
            link(g.memset(mask0[:, :], 0.0))
            g.memset(mask0[0:CHUNK, CHUNK:P], OFF).then_inc(const_made, 1)

            def sum_squares(base):
                for j in range(KT):
                    pool.wait_ge(sq_ready, base + j + 1)
                    if j == 0:
                        ins = g.tensor_copy(ssacc[:, 0:TOK], sq[:, j % 2, :])
                    else:
                        pool.wait_ge(ss_added, base + j)
                        ins = g.tensor_tensor(ssacc[:, 0:TOK], ssacc[:, 0:TOK], sq[:, j % 2, :], ALU.add)
                    ins.then_inc(ss_added, 1)

            def newton(y, m):
                link(g.tensor_tensor(nw[:, :], y[:, :], y[:, :], ALU.mult))
                link(g.tensor_tensor(nw[:, :], nw[:, :], m[:, :], ALU.mult))
                link(g.tensor_scalar(nw[:, :], nw[:, :], -0.5, 1.5, ALU.mult, ALU.add))

            def rope(buf, base, heads, width, half, rows, ts, table):
                nt = ts.stop - ts.start
                v = buf[0:rows, ts, base:base + heads * width].rearrange("p t (h d) -> p t h d", h=heads)
                ta = ra[0:rows, ts, 0:heads * 2 * half].rearrange("p t (h d) -> p t h d", h=heads)
                tb = rb[0:rows, ts, 0:heads * 2 * half].rearrange("p t (h d) -> p t h d", h=heads)

                def tab(a, b):
                    return rope_t[0:rows, ts, table + a:table + b].rearrange("p t (o d) -> p t o d", o=1)\
                        .broadcast_to([rows, nt, heads, b - a])
                g.tensor_tensor(ta, v[:, :, :, 0:2 * half], tab(0, 2 * half), ALU.mult)
                g.tensor_tensor(tb[:, :, :, 0:half], v[:, :, :, half:2 * half], tab(2 * half, 3 * half), ALU.mult)
                link(g.tensor_tensor(tb[:, :, :, half:2 * half], v[:, :, :, 0:half], tab(3 * half, 4 * half), ALU.mult))
                link(g.tensor_tensor(v[:, :, :, 0:2 * half], ta, tb, ALU.add))

            parts = [(P, slice(0, NPT)), (DEC, slice(SMP, NT))]
            sum_squares(0)
            for l in range(DEPTH):
                pool.wait_ge(root_ready, 2 * l + 1)
                newton(r, ms)
                g.tensor_tensor(r[:, :], r[:, :], nw[:, :], ALU.mult).then_inc(r_ready, 1)
                pool.wait_ge(small_in, 16 * 5 * (l + 1))
                g.tensor_copy(cache_ki4[:, :, :], cache_ki[:, :].rearrange("p (o d) -> p o d", o=1).broadcast_to([P, 4, ID]))
                pool.wait_ge(const_in, 16 * 5)
                pool.wait_ge(small_evac, l + 1)
                pool.wait_ge(proj_evac, 4 * NT * l + NT)
                for rows, ts in parts:
                    rope(z, Z_K, NKV, HD, RH, rows, ts, 0)
                    rope(z, Z_QI, NIH + 1, ID, RI, rows, ts, 4 * RH)
                for rows, ts in parts:
                    g.tensor_copy(ki4[0:rows, ts, :].rearrange("p t (o d) -> p t o d", o=4),
                                  z[0:rows, ts, Z_KI:Z_KI + ID].rearrange("p t (o d) -> p t o d", o=1)
                                  .broadcast_to([rows, ts.stop - ts.start, 4, ID]))
                    last = g.tensor_scalar(wi[0:rows, ts, :], z[0:rows, ts, Z_WI:Z_WI + NIH],
                                           float(ID) ** -0.5 * float(NIH) ** -0.5, None, ALU.mult)
                last.then_inc(roped, 1)
                pool.wait_ge(proj_evac, 4 * NT * l + 2 * NT)
                for rows, ts in parts:
                    rope(q, 0, NH, HD, RH, rows, ts, 0)
                g.memset(m8[:, 0, :], 0.0).then_inc(q_roped, 1)
                for i in range(NX):
                    t, hh = INDEX[i]
                    S, rows = KEYS[t], ROWS[t]
                    pool.wait_ge(scaled, NX * l + i + 1)
                    if hh == 0:
                        ins = g.tensor_copy(score[t][0:rows, :], rl[0:rows, i % 3, 0:S])
                    else:
                        pool.wait_ge(idx_acc, NX * l + i)
                        ins = g.tensor_tensor(score[t][0:rows, :], score[t][0:rows, :], rl[0:rows, i % 3, 0:S], ALU.add)
                    ins.then_inc(idx_acc, 1)
                pool.wait_ge(root_ready, 2 * l + 2)
                newton(rv, mv)
                g.tensor_tensor(rv[:, :], rv[:, :], nw[:, :], ALU.mult).then_inc(rv_ready, 1)
                for a, t in enumerate(TILE_ORDER):
                    pool.wait_ge(proj_evac, 4 * NT * (l + 1))
                    pool.wait_ge(mix_evac, NT * l + a + 1)
                    g.tensor_tensor(ug[0:ROWS[t], t, :], ug[0:ROWS[t], t, :], mb[0:ROWS[t], a % 2, :], ALU.mult)\
                        .then_inc(bm_ready, 1)
                sum_squares(KT * (2 * l + 1))
                sum_squares(KT * (2 * l + 2))
            pool.wait_ge(root_ready, 2 * DEPTH + 1)
            newton(r, ms)
            g.tensor_tensor(r[:, :], r[:, :], nw[:, :], ALU.mult).then_inc(r_ready, 1)

        @block.scalar
        def _(act):
            s = nc.scalar

            for t in range(NT):
                for half in range(2):
                    act.wait_ge(xT_done, 2 * t + half + 1)
                    s.activation(x[:, 4 * half:4 * half + 4, cols(t)],
                                 bank[2 * (t % 2) + half][:, 0:4 * ROWS[t]].rearrange("p (k n) -> p k n", k=4),
                                 ACT.Copy).then_inc(xT_evac, 1)
            def split_hi(n):
                act.wait_ge(w_ready[n % NRAW], raw_use(n))
                if n >= NSLOT:
                    act.wait_ge(*last_reader(n - NSLOT))
                s.activation(ring_hi[:, n % NSLOT, :], ring_raw[:, n % NRAW, :], ACT.Copy).then_inc(hi_ready, 1)

            def feed(j, stage):
                base = KT * stage
                if stage % 2:
                    act.wait_ge(y_read, KT * (GROUPS + 1) * (stage // 2) + j + 1)
                else:
                    act.wait_ge(x_ready, KT * GROUPS * (stage // 2) + j + 1)
                if base + j >= 2:
                    act.wait_ge(ss_added, base + j - 1)
                s.activation(sq[:, j % 2, :], x[:, j, :], ACT.Square).then_inc(sq_ready, 1)
                if stage < 2 * DEPTH:
                    s.activation(xh[:, j, :], x[:, j, :], ACT.Copy, scale=gain(stage, j)).then_inc(xh_ready, 1)

            act.wait_ge(g_ready, 1)
            for n in range(NSLOT):
                split_hi(n)
            for j in range(KT):
                feed(j, 0)
            for l in range(DEPTH):
                N0 = SLOTS * l
                act.wait_ge(ws_in, 16 * (l + 1))
                if l:
                    act.wait_ge(small_done, l)
                s.activation(w_small_r[:, :, 0, :], w_small[:, :, :], ACT.Copy).then_inc(ws_hi, 1)

                def evac(c, t):
                    act.wait_ge(proj_done, NT * (4 * l + c) + t + 1)
                    rows, src = ROWS[t], bank[t]
                    if c == QQ and t == 0:
                        act.wait_ge(small_evac, l + 1)
                    if c == KVQI:
                        dst = z[0:rows, t, 0:CW]
                    elif c == GV:
                        dst = gvn[0:rows, t, :]
                    elif c == UU:
                        dst = ug[0:rows, t, :]
                    if c == QQ:
                        s.activation(q[0:rows, t, :].rearrange("p (b j d) -> p j b d", j=2, d=HD),
                                     src[0:rows, :].rearrange("p (j b d) -> p j b d", j=2, d=HD),
                                     ACT.Copy, scale=r[0:rows, t:t + 1]).then_inc(proj_evac, 1)
                    else:
                        s.activation(dst, src[0:rows, :], ACT.Copy if c == KVQI else ACT.Gelu_apprx_tanh,
                                     scale=r[0:rows, t:t + 1]).then_inc(proj_evac, 1)

                def gating_square(t):
                    act.wait_ge(proj_evac, NT * (4 * l + GV) + t + 1)
                    act.wait_ge(q_roped, l + 1)
                    if t >= 2:
                        act.wait_ge(gv_sq, NT * l + t - 1)
                    s.activation(gsq[0:ROWS[t], t % 2, :], gvn[0:ROWS[t], t, :], ACT.Square,
                                 accum_out=ssv[0:ROWS[t], t:t + 1]).then_inc(gv_sq, 1)

                def index_relu(i):
                    ti, hh = INDEX[i]
                    act.wait_ge(idx_done, NX * l + i + 1)
                    if i >= 3:
                        act.wait_ge(idx_acc, NX * l + i - 2)
                    s.activation(rl[0:ROWS[ti], i % 3, 0:KEYS[ti]], bank[5 + i % 2][0:ROWS[ti], 0:KEYS[ti]],
                                 ACT.Relu).then_inc(idx_relu, 1)

                def index_scale(i):
                    ti, hh = INDEX[i]
                    act.wait_ge(idx_relu, NX * l + i + 1)
                    v = rl[0:ROWS[ti], i % 3, 0:KEYS[ti]]
                    s.activation(v, v, ACT.Copy, scale=wi[0:ROWS[ti], ti, hh:hh + 1]).then_inc(scaled, 1)

                def tr_high(n):
                    act.wait_ge(tr_done, (NTR + 2) * l + n + 1)
                    dst, width = index_parts[n - 4][0], index_parts[n - 4][2]
                    s.activation(dst, bank[7][:, 0:width], ACT.Copy).then_inc(tr_hi, 1)

                for n in range(S_OUT):
                    c, k = divmod(n, QUARTERS)
                    if n:
                        split_hi(N0 + n + NSLOT - 1)
                    if n == 1:
                        act.wait_ge(ms_ready, l + 1)
                        s.activation(r[:, :], r[:, :], ACT.Sqrt).then_inc(root_ready, 1)
                        act.wait_ge(r_ready, l + 1)
                    for t in range(NT):
                        if k == QUARTERS - 1:
                            evac(c, t)
                            if c == GV and t:
                                gating_square(t - 1)
                        if n == QUARTERS * UU and t == 0:
                            gating_square(NT - 1)
                        for kind, i in aux_after(n, t):
                            if kind == "index":
                                index_relu(i)
                                if i:
                                    index_scale(i - 1)
                                if i == NX - 1:
                                    index_scale(i)
                            elif 4 <= i < 8:
                                tr_high(i)
                split_hi(N0 + S_OUT + NSLOT - 1)

                def exp(i):
                    t, hh = ITEMS[i]
                    act.wait_ge(masked, NI * l + i + 1)
                    if i >= 2:
                        act.wait_ge(pT_done, NI * l + i - 1)
                    s.activation(pr[0:ROWS[t], i % 2, 0:KEYS[t]], L[0:ROWS[t], i % 3, 0:KEYS[t]], ACT.Exp,
                                 scale=-1.0, bias=nmax[0:ROWS[t], i:i + 1],
                                 accum_out=rsum[0:ROWS[t], i:i + 1]).then_inc(exp_done, 1)

                def pT_copy(i):
                    t, hh = ITEMS[i]
                    act.wait_ge(pT_done, NI * l + i + 1)
                    if i >= 2:
                        act.wait_ge(o_item, NI * l + i - 1)
                    n = -(-KEYS[t] // P) * ROWS[t]
                    if t == SMP:
                        s.activation(pT[:, i % 2, 0:DEC], bank[2 + i % 2][:, 0:DEC], ACT.Copy)
                        s.activation(pT[0:DEC, i % 2, DEC:2 * DEC], bank[2 + i % 2][0:DEC, DEC:2 * DEC],
                                     ACT.Copy).then_inc(pT_evac, 1)
                    else:
                        s.activation(pT[:, i % 2, 0:n], bank[2 + i % 2][:, 0:n], ACT.Copy).then_inc(pT_evac, 1)

                def mt_copy(a, part):
                    t = TILE_ORDER[a]
                    act.wait_ge(mt_done, 2 * NT * l + 2 * a + part + 1)
                    k0 = 0 if part == 0 else KT // 2
                    s.activation(vh[:, k0:k0 + 4, cols(t)], bank[7 - part][:, 0:4 * ROWS[t]].rearrange("p (k n) -> p k n", k=4),
                                 ACT.Copy).then_inc(vh_ready, 1)

                act.wait_ge(mv_ready, l + 1)
                s.activation(rv[:, :], rv[:, :], ACT.Sqrt).then_inc(root_ready, 1)
                exp(0)
                act.wait_ge(idx_acc, NX * (l + 1))
                for i in range(NI):
                    if i + 1 < NI:
                        exp(i + 1)
                    pT_copy(i)
                    if i % NH == 5 and i > NH:
                        mt_copy(i // NH - 1, 0)
                        mt_copy(i // NH - 1, 1)
                mt_copy(NT - 1, 0)
                mt_copy(NT - 1, 1)
                for j in range(KT):
                    feed(j, 2 * l + 1)
                    split_hi(N0 + S_OUT + j + NSLOT)
                for u in range(KT, UNITS):
                    g, f = divmod(u - KT, 2 * KT)
                    if f < KT:
                        f += KT * g
                        act.wait_ge(unit_done, UNITS * l + u + 1)
                        if f >= 2:
                            act.wait_ge(vl_ready, (2 * NT + FT) * l + 2 * NT + f - 1)
                        for half in range(2):
                            last = s.activation(rl2[:, f % 2, HALVES[half]], bank[2 * (u % 4) + half][:, 0:HALF], ACT.Relu)
                        last.then_inc(f1_relu, 1)
                        act.wait_ge(f1_relu, FT * l + f + 1)
                        s.activation(vh[:, f % KT, :], rl2[:, f % 2, :], ACT.Square).then_inc(vh_ready, 1)
                    elif g == GROUPS - 1:
                        feed(u % KT, 2 * l + 2)
                    if l < DEPTH - 1 or u < UNITS - NSLOT:
                        split_hi(N0 + S_OUT + u + NSLOT)
            act.wait_ge(ms_ready, DEPTH + 1)
            s.activation(r[:, :], r[:, :], ACT.Sqrt).then_inc(root_ready, 1)
            act.wait_ge(r_ready, DEPTH + 1)
            for t in range(NT):
                for half in range(2):
                    n = 2 * t + half
                    act.wait_ge(fin_done, n + 1)
                    s.activation(out_b[0:ROWS[t], t, half * 512:(half + 1) * 512], bank[n % 4][0:ROWS[t], :], ACT.Copy,
                                 scale=r[0:ROWS[t], t:t + 1]).then_inc(fin_evac, 1)

        @block.vector
        def _(dve):
            v = nc.vector
            count = [0]

            def link(ins):
                count[0] += 1
                ins.then_inc(dve_step, 1)
                dve.wait_ge(dve_step, count[0])

            def split_lo(n):
                dve.wait_ge(hi_ready, n + 1)
                v.tensor_tensor(ring_lo[:, n % NSLOT, :], ring_raw[:, n % NRAW, :], ring_hi[:, n % NSLOT, :].bitcast(F32),
                                ALU.subtract).then_inc(lo_ready, 1)

            def feed(j, base, stage):
                dve.wait_ge(xh_ready, base + j + 1)
                v.scalar_tensor_tensor(xl[:, j, :], x[:, j, :], gain(stage, j), xh[:, j, :].bitcast(F32),
                                       ALU.mult, ALU.subtract).then_inc(xl_ready, 1)

            def row_mean(n):
                dve.wait_ge(ss_done, n + 1)
                link(v.tensor_scalar(ms[:, :], bank[5][:, 0:NT], 1.0 / D, EPS, ALU.mult, ALU.add))
                v.reciprocal(r[:, :], ms[:, :]).then_inc(ms_ready, 1)

            dve.wait_ge(gT_done, 1)
            v.tensor_copy(gcol[:, :], bank[7][:, 0:7 * KT]).then_inc(g_ready, 1)
            dve.wait_ge(g_ready, 1)
            dve.wait_ge(xT_evac, 2 * NT)
            v.memset(m8[:, 1, :], 0.0).then_inc(x_ready, KT)
            for n in range(NSLOT):
                split_lo(n)
            for j in range(KT):
                feed(j, 0, 0)
            for l in range(DEPTH):
                N0 = SLOTS * l
                dve.wait_ge(ws_hi, l + 1)
                v.tensor_tensor(w_small_r[:, :, 1, :], w_small[:, :, :], w_small_r[:, :, 0, :].bitcast(F32), ALU.subtract)\
                    .then_inc(ws_split, 1)
                def small_copy():
                    dve.wait_ge(r_ready, l + 1)
                    dve.wait_ge(small_done, l + 1)
                    src = bank[5][:, 0:NT * 2 * NSM].rearrange("p (t a n) -> p t a n", t=NT, a=2)
                    for k in range(2):
                        for rows, ts in ((P, slice(0, NPT)), (DEC, slice(SMP, NT))):
                            nt = ts.stop - ts.start
                            rr = r[0:rows, ts].rearrange("p (t o) -> p t o", o=1).broadcast_to([rows, nt, NSM])
                            dst = z[0:rows, ts, CW:ZW] if k == 0 else zs2[0:rows, ts, :]
                            last = v.tensor_tensor(dst, src[0:rows, ts, k, :], rr, ALU.mult)
                    link(last)
                    for rows, ts in ((P, slice(0, NPT)), (DEC, slice(SMP, NT))):
                        last = v.tensor_tensor(z[0:rows, ts, CW:ZW], z[0:rows, ts, CW:ZW], zs2[0:rows, ts, :], ALU.add)
                    last.then_inc(small_evac, 1)

                dst = [kT, kTs]
                width = [SEQ, PAST + DEC]

                def tr_copy(n):
                    dve.wait_ge(tr_done, (NTR + 2) * l + n + 1)
                    if n < 2:
                        out, src = w_spT[:, 4 * n:4 * n + 4, :], bank[7][:, :].rearrange("p (g n) -> p g n", g=4)
                    elif n < 4:
                        out, src = dst[n - 2], bank[7][:, 0:width[n - 2]]
                    elif n < 8:
                        dve.wait_ge(tr_hi, 4 * l + n - 3)
                        hi, lo, w = index_parts[n - 4]
                        v.tensor_tensor(lo, bank[7][:, 0:w], hi.bitcast(F32), ALU.subtract).then_inc(tr_evac, 1)
                        return
                    elif n < 12:
                        out, src = qT[:, n - 8, 0:SEQ], bank[7][:, :]
                    else:
                        out, src = qT[:, :, SEQ:TOK], bank[7][:, 0:4 * DEC].rearrange("p (b n) -> p b n", b=4)
                    v.tensor_copy(out, src).then_inc(tr_evac, 1)
                    if n == 1:
                        dve.wait_ge(tr_evac, (NTR + 2) * l + 2)
                        v.memset(w_spT[CHUNK:P, :, 0:CHUNK], 0.0).then_inc(spT_ready, 1)

                def topk_round(t, n):
                    rows = ROWS[t]
                    link(v.max(m8[0:rows, 1, :], score[t][0:rows, :]))
                    link(v.match_replace(score[t][0:rows, :], m8[0:rows, 1, :], score[t][0:rows, :], TAKEN))

                def mask_of(t):
                    rows = ROWS[t]
                    link(v.tensor_scalar(score[t][0:rows, :], score[t][0:rows, :], SPLIT, OFF, ALU.is_gt, ALU.mult))

                def rounds(t):
                    return (TOP_S if t == SMP else TOP_P) // 8

                def masked_logits(i):
                    t, hh = ITEMS[i]
                    rows, S = ROWS[t], KEYS[t]
                    dve.wait_ge(qk_done, NI * l + i + 1)
                    if i >= 3:
                        dve.wait_ge(exp_done, NI * l + i - 2)
                    mk = mask0[0:rows, :] if t == 0 else score[t][0:rows, :]
                    v.tensor_tensor_reduce(out=L[0:rows, i % 3, 0:S], in0=bank[i % 2][0:rows, 0:S], in1=mk,
                                           scale=-SCALE, scalar=3e38, op0=ALU.add, op1=ALU.min,
                                           accum_out=nmax[0:rows, i:i + 1]).then_inc(masked, 1)

                def gv_norm(t):
                    v.scalar_tensor_tensor(gvn[0:ROWS[t], t, :], gvn[0:ROWS[t], t, :], rv[0:ROWS[t], t:t + 1],
                                           gate_bc[0:ROWS[t], :], ALU.mult, ALU.mult).then_inc(gvn_ready, 1)

                def mix_copy(a):
                    t = TILE_ORDER[a]
                    dve.wait_ge(mix_done, NT * l + a + 1)
                    if a >= 2:
                        dve.wait_ge(bm_ready, NT * l + a - 1)
                    c0 = (2 * DEPTH + 1) * KT + l * NG
                    v.tensor_tensor(mb[0:ROWS[t], a % 2, :].rearrange("p (g c) -> p g c", g=NG),
                                    bank[6][0:ROWS[t], :].rearrange("p (g c) -> p g c", g=NG),
                                    gcol[0:ROWS[t], c0:c0 + NG].rearrange("p (g o) -> p g o", o=1)
                                    .broadcast_to([ROWS[t], NG, CPG]), ALU.add).then_inc(mix_evac, 1)

                def o_copy(a):
                    t = TILE_ORDER[a]
                    rows = ROWS[t]
                    dve.wait_ge(o_item, NI * l + NH * (a + 1))
                    link(v.reciprocal(rinv[0:rows, NH * a:NH * (a + 1)], rsum[0:rows, NH * a:NH * (a + 1)]))
                    v.tensor_tensor(o[0:rows, a % 2, :].rearrange("p (h d) -> p h d", h=NH),
                                    bank[4 + a % 2][0:rows, :].rearrange("p (h d) -> p h d", h=NH),
                                    rinv[0:rows, NH * a:NH * (a + 1)].rearrange("p (h o) -> p h o", o=1)
                                    .broadcast_to([rows, NH, HD]), ALU.mult).then_inc(o_ready, 1)

                def mt_low(a, part):
                    t = TILE_ORDER[a]
                    n = (2 * NT + FT) * l + 2 * a + part + 1
                    dve.wait_ge(vh_ready, n)
                    k0 = 0 if part == 0 else KT // 2
                    v.tensor_tensor(vl[:, k0:k0 + 4, cols(t)], bank[7 - part][:, 0:4 * ROWS[t]].rearrange("p (k n) -> p k n", k=4),
                                    vh[:, k0:k0 + 4, cols(t)].bitcast(F32), ALU.subtract).then_inc(vl_ready, 1)

                todo = [(t, n) for t in INDEX_TILES for n in range(rounds(t))]

                def topk_next():
                    t, n = todo.pop(0)
                    if n == 0:
                        dve.wait_ge(idx_acc, NX * l + NIH * (INDEX_TILES.index(t) + 1))
                        if t != SMP:
                            link(v.memset(score[t][0:CHUNK, KEYS[t] - CHUNK:KEYS[t]], NEG))
                    topk_round(t, n)
                    if n == rounds(t) - 1:
                        mask_of(t)

                for n in range(S_OUT):
                    if n:
                        split_lo(N0 + n + NSLOT - 1)
                    if n == 1:
                        row_mean(l)
                    if n == 4:
                        small_copy()
                    for t in range(NT):
                        for kind, i in aux_after(n, t):
                            if kind == "tr":
                                tr_copy(i)
                        g = n * NT + t
                        if todo and (todo[0][1] or g >= INDEX_AT + NIH * (INDEX_TILES.index(todo[0][0]) + 1) + 1):
                            topk_next()
                split_lo(N0 + S_OUT + NSLOT - 1)
                dve.wait_ge(gv_sq, NT * (l + 1))
                link(v.tensor_scalar(mv[:, :], ssv[:, :], 1.0 / DB, EPS, ALU.mult, ALU.add))
                v.reciprocal(rv[:, :], mv[:, :]).then_inc(mv_ready, 1)
                dve.wait_ge(rv_ready, l + 1)
                for t in range(NT):
                    gv_norm(t)
                dve.wait_ge(idx_acc, NX * (l + 1))
                for i in range(NI):
                    a, t = i // NH, ITEMS[i][0]
                    while any(x_[0] == t for x_ in todo):
                        topk_next()
                    if todo:
                        topk_next()
                    masked_logits(i)
                    if i % NH == 3 and a:
                        o_copy(a - 1)
                    if i % NH == 4:
                        mix_copy(a)
                    if i % NH == 7 and a:
                        mt_low(a - 1, 0)
                        mt_low(a - 1, 1)
                o_copy(NT - 1)

                mt_low(NT - 1, 0)
                mt_low(NT - 1, 1)
                for j in range(KT):
                    dve.wait_ge(unit_done, UNITS * l + j + 1)
                    b = 2 * (j % 4)
                    for half in range(2):
                        last = v.tensor_tensor(x[:, j, HALVES[half]], x[:, j, HALVES[half]], bank[b + half][:, 0:HALF], ALU.add)
                    last.then_inc(y_read, 1)
                    if j:
                        feed(j - 1, KT * (2 * l + 1), 2 * l + 1)
                    split_lo(N0 + S_OUT + j + NSLOT)
                feed(KT - 1, KT * (2 * l + 1), 2 * l + 1)
                for u in range(KT, UNITS):
                    g, f = divmod(u - KT, 2 * KT)
                    b = 2 * (u % 4)
                    if f < KT:
                        f += KT * g
                        if f == 0:
                            dve.wait_ge(kv_out, 16 * KV_OUTS * (l + 1))
                        dve.wait_ge(f1_relu, FT * l + f + 1)
                        link(v.tensor_tensor(h32[:, f % 2, :], rl2[:, f % 2, :], rl2[:, f % 2, :], ALU.mult))
                        dve.wait_ge(vh_ready, (2 * NT + FT) * l + 2 * NT + f + 1)
                        v.tensor_tensor(vl[:, f % KT, :], h32[:, f % 2, :], vh[:, f % KT, :].bitcast(F32), ALU.subtract)\
                            .then_inc(vl_ready, 1)
                    else:
                        j = f - KT
                        n = KT * (GROUPS * l + g) + j
                        dve.wait_ge(unit_done, UNITS * l + u + 1)
                        for half in range(2):
                            last = v.tensor_tensor(yb[:, j % 2, HALVES[half]], r2b[:, HALVES[half]], bank[b + half][:, 0:HALF],
                                                   ALU.mult)
                        last.then_inc(y_read, 1)
                        dve.wait_ge(y_read, KT * (GROUPS + 1) * l + KT * (g + 1) + j + 1)
                        v.tensor_tensor(x[:, j, :], x[:, j, :], yb[:, j % 2, :], ALU.add).then_inc(x_ready, 1)
                        if g == GROUPS - 1 and j and l < DEPTH - 1:
                            feed(j - 1, KT * (2 * l + 2), 2 * l + 2)
                    if l < DEPTH - 1 or u < UNITS - NSLOT:
                        split_lo(N0 + S_OUT + u + NSLOT)
                    if u == KT + 1:
                        dve.wait_ge(ssb_done, l + 1)
                        for half in range(2):
                            last = v.tensor_scalar(r2b[:, HALVES[half]], bank[6 + half][:, 0:HALF], 1.0 / D, EPS,
                                                   ALU.mult, ALU.add)
                        last.then_inc(ssb_read, 1)
                        dve.wait_ge(ssb_read, l + 1)
                        link(v.reciprocal(r2b[:, :], r2b[:, :]))
                if l < DEPTH - 1:
                    feed(KT - 1, KT * (2 * l + 2), 2 * l + 2)
            for j in range(KT):
                dve.wait_ge(sq_ready, KT * 2 * DEPTH + j + 1)
                v.tensor_scalar(x[:, j, :], x[:, j, :], gain(2 * DEPTH, j), None, ALU.mult).then_inc(y_scaled, 1)
            row_mean(DEPTH)

        @block.tensor
        def _(pe):
            mm = nc.tensor.matmul
            tp = nc.tensor.transpose

            def row_sums(n):
                pe.wait_ge(ss_added, KT * (2 * n + 1))
                for t in range(NT):
                    last = mm(bank[5][:, t:t + 1], ssacc[:, t * P:(t + 1) * P], ones[:, 0:1], start=True, stop=True)
                last.then_inc(ss_done, 1)

            pe.wait_ge(const_made, 5)
            pe.wait_ge(const_in, 16 * 5)
            tp(bank[7][:, 0:7 * KT], grow[:, :], ident[0:7 * KT, 0:7 * KT]).then_inc(gT_done, 1)
            pe.wait_ge(x_loaded, 32)
            for t in range(NT):
                for half in range(2):
                    if t >= 2:
                        pe.wait_ge(xT_evac, 2 * t + half - 3)
                    for k in range(4):
                        last = tp(bank[2 * (t % 2) + half][:, k * ROWS[t]:(k + 1) * ROWS[t]],
                                  x_in[0:ROWS[t], t, (4 * half + k) * P:(4 * half + k + 1) * P],
                                  ident[0:ROWS[t], 0:ROWS[t]])
                    last.then_inc(xT_done, 1)

            for l in range(DEPTH):
                def slot(n):
                    pe.wait_ge(lo_ready, SLOTS * l + n + 1)
                    return tuple(b[:, n % NSLOT, :] for b in (ring_hi, ring_lo))

                def group(n, t, w):
                    c, k = divmod(n, QUARTERS)
                    if k == 0 and c:
                        pe.wait_ge(proj_evac, NT * (4 * l + c - 1) + t + 1)
                    elif n == 0 and l:
                        pe.wait_ge(*unit_read(UNITS * l - 4 + t // 2))
                    wh, wl = (b.rearrange("p (k n) -> p k n", k=KQ) for b in w)
                    for kk in range(KQ):
                        kx = KQ * k + kk
                        for a, b in ((xh, wh), (xh, wl), (xl, wh)):
                            last = mm(bank[t][0:ROWS[t], :], a[:, kx, cols(t)], b[:, kk, :],
                                      start=kx == 0 and b is wh and a is xh, stop=kx == KT - 1 and a is xl)
                    if k == QUARTERS - 1:
                        last.then_inc(proj_done, 1)
                    elif t == NT - 1:
                        last.then_inc(quarter_done, 1)

                def index(i):
                    t, hh = INDEX[i]
                    if i == 0:
                        pe.wait_ge(tr_evac, (NTR + 2) * l + 8)
                    if i >= 2:
                        pe.wait_ge(idx_relu, NX * l + i - 1)
                    b, rows = 32 * (hh % 4), ROWS[t]
                    kh, kl = (kish, kisl) if t == SMP else (kih, kil)
                    for a, k in ((qih, kh), (qih, kl), (qil, kh)):
                        last = mm(bank[5 + i % 2][0:rows, 0:KEYS[t]], a[b:b + ID, hh // 4, cols(t)], k[b:b + ID, 0:KEYS[t]],
                                  start=a is qih and k is kh, stop=a is qil)
                    last.then_inc(idx_done, 1)

                tr = [0]

                def tr_group(parts):
                    n = (NTR + 2) * l + tr[0]
                    if n:
                        pe.wait_ge(tr_evac, n)
                    c0 = 0
                    for src in parts:
                        rows = src.shape[0]
                        last = tp(bank[7][:, c0:c0 + rows], src, ident[0:rows, 0:rows])
                        c0 += rows
                    last.then_inc(tr_done, 1)
                    tr[0] += 1

                zz = lambda t, a, b: z[0:ROWS[t], t, a:b]
                tr_parts = [[w_sp[:, 4 * n + g, :] for g in range(4)] for n in range(2)]
                tr_parts += [[zz(t, Z_K, Z_K + DKV) for t in range(NPT)],
                             [cache_k[:, :], zz(SMP, Z_K, Z_K + DKV)],
                             [ki4[:, t, :] for t in range(NPT)],
                             [cache_ki4[:, :, :].rearrange("p a d -> p (a d)"), ki4[0:DEC, SMP, :]]]
                tr_parts += [[zz(t, Z_QI + b * P, Z_QI + (b + 1) * P) for t in list(range(1, NPT)) + [SMP]] for b in range(2)]
                tr_parts += [[q[:, t, b * P:(b + 1) * P] for t in range(NPT)] for b in range(4)]
                tr_parts += [[q[0:DEC, SMP, b * P:(b + 1) * P] for b in range(4)]]

                for n in range(S_OUT):
                    w = slot(n)
                    if n < QUARTERS:
                        pe.wait_ge(xl_ready, KT * 2 * l + KQ * (n + 1))
                    for t in range(NT):
                        group(n, t, w)
                        for kind, i in aux_after(n, t):
                            if kind == "tr":
                                if i == 0:
                                    pe.wait_ge(small_in, 16 * 5 * (l + 1))
                                if i == 2:
                                    pe.wait_ge(roped, l + 1)
                                if i == 8:
                                    pe.wait_ge(q_roped, l + 1)
                                tr_group(tr_parts[i])
                            else:
                                index(i)
                    if n == 0:
                        row_sums(l)
                    if n == QUARTERS - 1:
                        pe.wait_ge(ws_split, l + 1)
                        pe.wait_ge(ms_ready, l + 1)
                        for t in range(NT):
                            c0 = 2 * NSM * t
                            for k in range(KT):
                                both = (xh, w_small_r[:, k, :, :].rearrange("p a n -> p (a n)"), 2 * NSM)
                                high = (xl, w_small_r[:, k, 0, :], NSM)
                                for m, (a, w_, n_) in enumerate((high, both) if k == KT - 1 else (both, high)):
                                    last = mm(bank[5][0:ROWS[t], c0:c0 + n_], a[:, k, cols(t)], w_,
                                              start=k == 0 and m == 0, stop=k == KT - 1 and m == 1)
                        last.then_inc(small_done, 1)

                def scores_of(i):
                    t, hh = ITEMS[i]
                    if i == 0:
                        pe.wait_ge(tr_evac, (NTR + 2) * (l + 1))
                        pe.wait_ge(proj_evac, 4 * NT * (l + 1))
                        pe.wait_ge(idx_relu, NX * (l + 1))
                    if i >= 2:
                        pe.wait_ge(masked, NI * l + i - 1)
                    b = HD * (hh // 4)
                    keys = kTs if t == SMP else kT
                    mm(bank[i % 2][0:ROWS[t], 0:KEYS[t]], qT[b:b + HD, hh % 4, cols(t)], keys[b:b + HD, 0:KEYS[t]],
                       start=True, stop=True).then_inc(qk_done, 1)

                def p_transpose(i):
                    t, hh = ITEMS[i]
                    pe.wait_ge(exp_done, NI * l + i + 1)
                    if i >= 2:
                        pe.wait_ge(pT_evac, NI * l + i - 1)
                    for s0 in range(0, KEYS[t], P):
                        n = min(P, KEYS[t] - s0)
                        c0 = s0 // P * ROWS[t]
                        last = tp(bank[2 + i % 2][0:n, c0:c0 + ROWS[t]], pr[0:ROWS[t], i % 2, s0:s0 + n],
                                  ident[0:ROWS[t], 0:ROWS[t]])
                    last.then_inc(pT_done, 1)

                def weighted(i):
                    t, hh = ITEMS[i]
                    a = i // NH
                    pe.wait_ge(pT_evac, NI * l + i + 1)
                    if hh == 0 and a >= 2:
                        pe.wait_ge(o_ready, NT * l + a - 1)
                    nb = -(-KEYS[t] // P)
                    g0 = Z_V + HD * (hh // 4)
                    for s in range(nb):
                        n = min(P, KEYS[t] - s * P)
                        if t == SMP:
                            vals = cache_v[:, HD * (hh // 4):HD * (hh // 4) + HD] if s == 0 else z[0:DEC, SMP, g0:g0 + HD]
                        else:
                            vals = z[:, s, g0:g0 + HD]
                        last = mm(bank[4 + a % 2][0:ROWS[t], hh * HD:(hh + 1) * HD],
                                  pT[0:n, i % 2, s * ROWS[t]:(s + 1) * ROWS[t]], vals, start=s == 0, stop=s == nb - 1)
                    last.then_inc(o_item, 1)

                def spatial(a):
                    t = TILE_ORDER[a]
                    pe.wait_ge(spT_ready, l + 1)
                    pe.wait_ge(gvn_ready, NT * (l + 1))
                    if a >= 2:
                        pe.wait_ge(vl_ready, (2 * NT + FT) * l + 2 * (a - 1))
                    rows = ROWS[t]
                    for g in range(NG):
                        last = mm(bank[6][0:rows, g * CPG:(g + 1) * CPG], w_spT[0:rows, g, 0:rows],
                                  gvn[0:rows, t, g * CPG:(g + 1) * CPG], start=True, stop=True)
                    last.then_inc(mix_done, 1)

                def mt_group(a, part):
                    t = TILE_ORDER[a]
                    if a:
                        pe.wait_ge(vl_ready, (2 * NT + FT) * l + 2 * a)
                    if part:
                        pe.wait_ge(mix_evac, NT * l + min(a + 2, NT))
                    pe.wait_ge(o_ready if part == 0 else bm_ready, NT * l + a + 1)
                    src = o[0:ROWS[t], a % 2, :] if part == 0 else ug[0:ROWS[t], t, :]
                    for k in range(4):
                        last = tp(bank[7 - part][:, k * ROWS[t]:(k + 1) * ROWS[t]], src[:, k * P:(k + 1) * P],
                                  ident[0:ROWS[t], 0:ROWS[t]])
                    last.then_inc(mt_done, 1)

                scores_of(0)
                scores_of(1)
                for i in range(NI):
                    if i % NH == 2:
                        spatial(i // NH)
                    if i + 2 < NI:
                        scores_of(i + 2)
                    p_transpose(i)
                    if i:
                        weighted(i - 1)
                    if i % NH == 5 and i > NH:
                        mt_group(i // NH - 1, 0)
                        mt_group(i // NH - 1, 1)
                weighted(NI - 1)
                mt_group(NT - 1, 0)
                mt_group(NT - 1, 1)
                pe.wait_ge(vl_ready, (2 * NT + FT) * l + 2 * NT)
                for u in range(UNITS):
                    wh, wl = (b.rearrange("p (k n) -> p k n", k=KT) for b in slot(S_OUT + u))
                    g, f = divmod(u - KT, 2 * KT)
                    first_product = u >= KT and f < KT
                    ah, al = (xh, xl) if first_product else (vh, vl)
                    if u >= 4:
                        pe.wait_ge(*unit_read(UNITS * l + u - 4))
                    if u == KT + 3:
                        pe.wait_ge(ssb_read, l + 1)
                    for k in range(KT):
                        if u == KT:
                            pe.wait_ge(xl_ready, KT * (2 * l + 1) + k + 1)
                        if u >= KT and f == KT:
                            pe.wait_ge(vl_ready, (2 * NT + FT) * l + 2 * NT + KT * g + k + 1)
                        for w, a in ((wh, ah), (wh, al), (wl, ah)):
                            for half in range(2):
                                last = mm(bank[2 * (u % 4) + half][:, 0:HALF], w[:, k, :], a[:, k, HALVES[half]],
                                          start=k == 0 and w is wh and a is ah, stop=k == KT - 1 and w is wl)
                    last.then_inc(unit_done, 1)
                    if u == KT + 1:
                        pe.wait_ge(ss_added, KT * (2 * l + 2))
                        for half in range(2):
                            last = mm(bank[6 + half][:, 0:HALF], ones[:, :], ssacc[:, HALVES[half]], start=True, stop=True)
                        last.then_inc(ssb_done, 1)
            pe.wait_ge(y_scaled, KT)
            row_sums(DEPTH)
            for t in range(NT):
                for half in range(2):
                    n = 2 * t + half
                    if n >= 4:
                        pe.wait_ge(fin_evac, n - 3)
                    for k in range(4):
                        last = tp(bank[n % 4][0:ROWS[t], k * P:(k + 1) * P], x[:, 4 * half + k, cols(t)], ident[:, :])
                    last.then_inc(fin_done, 1)


_INS = ['x_prompt', 'x_sample', 'cache_k', 'cache_v', 'cache_kidx', 'norm_mix', 'w_in', 'gate_norm', 'w_spatial',
        'b_spatial', 'w_out', 'norm_ffn', 'w_ff1', 'w_ff2', 'norm_final']


def kernel(**inputs):
    import numpy as np
    import concourse.bacc as bacc
    from concourse import mybir
    from concourse.bass_utils import run_bass_kernel_spmd

    nc = bacc.Bacc("TRN2", target_bir_lowering=False, num_devices=1)
    arrays = {n: np.ascontiguousarray(inputs[n]) for n in _INS}
    L, B, past, nkv, hd = arrays['cache_k'].shape
    seq, d = arrays['x_prompt'].shape[1:]
    dec = arrays['x_sample'].shape[1]
    idd = arrays['cache_kidx'].shape[3]
    db = arrays['gate_norm'].shape[1]

    nt = seq // 128 + 1
    pos = np.arange(nt * 128).reshape(nt, 128).T.astype(np.float32)
    pos[:, nt - 1] = past + np.arange(128)
    parts = []
    for half in (hd // 8, idd // 8):
        inv = np.power(np.float32(500000.0), -np.arange(half, dtype=np.float32) * np.float32(2.0 / (2 * half)))
        ang = (pos[:, :, None] * inv.astype(np.float32)).astype(np.float32)
        c, s = np.cos(ang), np.sin(ang)
        parts += [c, c, -s, s]
    arrays['rope_table'] = np.concatenate(parts, -1).astype(np.float32)

    outs = {'y_prompt': (B, seq, d), 'y_sample': (B, dec, d), 'k_prompt': (L, B, seq, nkv, hd),
            'v_prompt': (L, B, seq, nkv, hd), 'kidx_prompt': (L, B, seq, idd), 'k_sample': (L, B, dec, nkv, hd),
            'v_sample': (L, B, dec, nkv, hd), 'kidx_sample': (L, B, dec, idd), 'gv_sample': (L, B, dec, db)}
    A = {n: nc.dram_tensor(f"in_{n}", a.shape, mybir.dt.from_np(a.dtype), kind="ExternalInput").ap()
         for n, a in arrays.items()}
    O = {n: nc.dram_tensor(f"out_{n}", s, mybir.dt.float32, kind="ExternalOutput").ap() for n, s in outs.items()}
    hybrid_encoder_program(nc, A, O)
    res = run_bass_kernel_spmd(nc, [{f"in_{n}": a for n, a in arrays.items()}], core_ids=[0])
    return tuple(res.results[0][f"out_{n}"] for n in outs)
```

```python
import concourse.bass as bass
from concourse import mybir
from contextlib import ExitStack
import numpy as np


def hybrid_encoder_program(nc, A, O):
    F32 = mybir.dt.float32
    F32R = mybir.dt.float32r
    ALU = mybir.AluOpType
    ACT = mybir.ActivationFunctionType

    P = 128
    SEQ, D = A["x_prompt"].shape[1], A["x_prompt"].shape[2]
    DEC = A["x_sample"].shape[1]
    DEPTH, _, PAST, NKV, HD = A["cache_k"].shape
    ID = A["cache_kidx"].shape[3]
    N_IN = A["w_in"].shape[2]
    DB = A["gate_norm"].shape[1]
    NG = A["w_spatial"].shape[1]
    DFF = A["w_ff1"].shape[2]
    DA = D - DB
    NH = DA // HD
    NIH = 8
    CHUNK = 64
    KT = D // P
    FT = DFF // P
    CPG = DB // NG
    DKV = NKV * HD
    TOP_P, TOP_S = min(256, SEQ // 4), min(256, (PAST + DEC) // 4)
    EPS = 1e-6
    NPT = SEQ // P
    NT = NPT + 1
    SMP = NPT
    TOK = SEQ + DEC
    HALF = TOK // 2
    HALVES = [slice(0, HALF), slice(HALF, TOK)]
    ROWS = [P] * NPT + [DEC]
    KEYS = [P * (t + 1) for t in range(NPT)] + [PAST + DEC]
    RH, RI = HD // 8, ID // 8
    NEG, TAKEN, SPLIT, OFF = -2e38, -3e38, -2.5e38, -1e30
    SCALE = float(HD) ** -0.5

    C_Q, C_K = 0, DA
    C_SMALL = DA + 2 * DKV + NIH * ID
    NSM = ID + NIH
    C_U = C_SMALL + NSM
    C_GV = C_U + DB
    CW = 512
    CHUNKS = [C_K, C_Q, C_GV, C_U]
    KVQI, QQ, GV, UU = range(4)
    ZW = CW + NSM
    Z_K, Z_V, Z_QI, Z_KI, Z_WI = 0, DKV, 2 * DKV, CW, CW + ID

    NRAW, NSLOT = 2, 4
    SW = KT * P
    QUARTERS = SW // CW and D // (SW // CW * P)
    KQ = SW // CW
    GROUPS = FT // KT
    S_OUT = QUARTERS * len(CHUNKS)
    S_FFN = S_OUT + KT
    UNITS = KT + 2 * KT * GROUPS
    SLOTS = S_FFN + 2 * KT * GROUPS

    TILE_ORDER = [0, 1, SMP] + list(range(2, NPT))
    ITEMS = [(t, h) for t in TILE_ORDER for h in range(NH)]
    NI = len(ITEMS)
    INDEX_TILES = TILE_ORDER[1:]
    INDEX = [(t, h) for t in INDEX_TILES for h in range(NIH)]
    NX = len(INDEX)

    def cols(t):
        return slice(t * P, t * P + ROWS[t])

    ctx = ExitStack()
    with ctx:
        def sb(name, shape, dt=F32):
            return ctx.enter_context(nc.sbuf_tensor(name, shape, dt))

        def sem(name):
            return ctx.enter_context(nc.semaphore(name))

        x = sb("x", [P, KT, TOK])
        ring_raw = sb("ring_raw", [P, NRAW, SW])
        ring_hi = sb("ring_hi", [P, NSLOT, SW], F32R)
        ring_lo = sb("ring_lo", [P, NSLOT, SW], F32R)
        w_small = sb("w_small", [P, KT, NSM])
        w_small_r = sb("w_small_r", [P, KT, 2, NSM], F32R)
        ident = sb("ident", [P, P])
        ones = sb("ones", [P, P])
        grow = sb("grow", [7 * KT, P])
        gcol = sb("gcol", [P, 7 * KT])
        rope_t = sb("rope_t", [P, NT, 4 * RH + 4 * RI])
        w_spT = sb("w_spT", [P, NG, P])
        gate_bc = sb("gate_bc", [P, DB])
        cache_k = sb("cache_k_t", [P, DKV])
        cache_v = sb("cache_v_t", [P, DKV])
        cache_ki = sb("cache_ki_t", [P, ID])
        cache_ki4 = sb("cache_ki4", [P, 4, ID])
        ssacc = sb("ssacc", [P, NT * P])
        ms = sb("ms", [P, NT])
        r = sb("r", [P, NT])
        ssv = sb("ssv", [P, NT])
        rv = sb("rv", [P, NT])
        mv = sb("mv", [P, NT])
        nw = sb("nw", [P, NT])
        wi = sb("wi", [P, NT, NIH])
        m8 = sb("m8", [P, NT, 8])
        mask0 = sb("mask0", [P, P])
        nmax = sb("nmax", [P, NI])
        rsum = sb("rsum", [P, NI])
        rinv = sb("rinv", [P, NI])
        z = sb("z", [P, NT, ZW])
        w_sp = sb("w_sp", [P, NG, P])
        gsq = sb("gsq", [P, 2, DB])

        class Area:
            def __init__(self, name, size):
                self.all, self.used = sb(name, [P, size]), 0

            def take(self, *dims):
                n = int(np.prod(dims))
                v = self.all[:, self.used:self.used + n]
                self.used += n
                assert self.used <= self.all.shape[1], self.used
                if len(dims) == 1:
                    return v
                if len(dims) == 2:
                    return v.rearrange("p (a b) -> p a b", a=dims[0])
                return v.rearrange("p (a b c) -> p a b c", a=dims[0], b=dims[1])

        late = Area("late", 2 * NT * DB + SEQ + PAST + DEC + sum(KEYS[1:]) + 4 * TOK)
        ug, gvn = late.take(NT, DB), late.take(NT, DB)
        kT, kTs = late.take(SEQ), late.take(PAST + DEC)
        at = late.used
        score = {t: late.take(KEYS[t]) for t in INDEX_TILES}
        late.used = at
        late.used = at + sum(KEYS[1:])
        qT = late.take(4, TOK)
        ki4 = qT[:, :, :].rearrange("p a b -> p (a b)")[:, 0:NT * 4 * ID].rearrange("p (t n) -> p t n", t=NT)
        late.used = 0
        sq, rl2, yb, h32 = (late.take(2, TOK) for _ in range(4))
        r2b = late.take(TOK)
        late.used = 0
        x_in = late.take(NT, D)
        out_b = x_in

        with ExitStack() as area:
            def sb(name, shape, dt=F32):
                return area.enter_context(nc.sbuf_tensor(name, shape, dt))
            att = Area("att", 3 * SEQ + 4 * SEQ + 2 * DA + 2 * DB)
            L, pr, pT = att.take(3, SEQ), att.take(2, SEQ), att.take(2, SEQ)
            o, mb = att.take(2, DA), att.take(2, DB)

        def sb(name, shape, dt=F32):
            return ctx.enter_context(nc.sbuf_tensor(name, shape, dt))
        xh = sb("xh", [P, KT, TOK], F32R)
        xl = sb("xl", [P, KT, TOK], F32R)

        with ExitStack() as area:
            def sb(name, shape, dt=F32):
                return area.enter_context(nc.sbuf_tensor(name, shape, dt))
            early = Area("early", NT * DA + 2 * NT * NH * 2 * RH + 3 * SEQ)
            q = early.take(NT, DA)
            ra, rb = early.take(NT, NH * 2 * RH), early.take(NT, NH * 2 * RH)
            small_fm = early.all[:, NT * NSM:NT * NSM + TOK]
            zs2 = early.all[:, 0:NT * NSM].rearrange("p (t n) -> p t n", t=NT)
            rl = early.take(3, SEQ)
            qih, qil = sb("qih", [P, 2, TOK], F32R), sb("qil", [P, 2, TOK], F32R)
            kih, kil = sb("kih", [P, SEQ], F32R), sb("kil", [P, SEQ], F32R)
            kish, kisl = sb("kish", [P, PAST + DEC], F32R), sb("kisl", [P, PAST + DEC], F32R)

        def sb(name, shape, dt=F32):
            return ctx.enter_context(nc.sbuf_tensor(name, shape, dt))
        vh = sb("vh", [P, KT, TOK], F32R)
        vl = sb("vl", [P, KT, TOK], F32R)

        bank = [ctx.enter_context(nc.psum_tensor(f"bank{i}", [P, 512], F32)) for i in range(8)]

        w_ready = [sem(f"w_ready{s}") for s in range(NRAW)]
        hi_ready, lo_ready = sem("hi_ready"), sem("lo_ready")
        ws_hi, ws_split = sem("ws_hi"), sem("ws_split")
        xh_ready, vh_ready, vl_ready = sem("xh_ready"), sem("vh_ready"), sem("vl_ready")
        tr_hi, scaled = sem("tr_hi"), sem("scaled")
        quarter_done, unit_done, y_read = sem("quarter_done"), sem("unit_done"), sem("y_read")
        y_scaled = sem("y_scaled")
        const_in, rope_in = sem("const_in"), sem("rope_in")
        x_in_ready = [sem(f"x_in_ready{t}") for t in range(NT)]
        small_in = sem("small_in")
        ws_in = sem("ws_in")
        const_made = sem("const_made")
        xT_done, xT_evac = sem("xT_done"), sem("xT_evac")
        gT_done, g_ready = sem("gT_done"), sem("g_ready")
        x_ready = sem("x_ready")
        sq_ready, ss_added = sem("sq_ready"), sem("ss_added")
        xl_ready = sem("xl_ready")
        ss_done, ms_ready, r_ready = sem("ss_done"), sem("ms_ready"), sem("r_ready")
        root_ready, mv_ready = sem("root_ready"), sem("mv_ready")
        proj_done, proj_evac = sem("proj_done"), sem("proj_evac")
        small_done, small_evac = sem("small_done"), sem("small_evac")
        small_fm_ready, small_tr = sem("small_fm_ready"), sem("small_tr")
        idx_roped, roped, q_roped = sem("idx_roped"), sem("roped"), sem("q_roped")
        tr_done, tr_evac = sem("tr_done"), sem("tr_evac")
        idx_done, idx_relu, idx_acc = sem("idx_done"), sem("idx_relu"), sem("idx_acc")
        gv_sq, rv_ready, gvn_ready = sem("gv_sq"), sem("rv_ready"), sem("gvn_ready")
        mix_done, mix_evac, bm_ready = sem("mix_done"), sem("mix_evac"), sem("bm_ready")
        qk_done, masked, exp_done = sem("qk_done"), sem("masked"), sem("exp_done")
        pT_done, pT_evac = sem("pT_done"), sem("pT_evac")
        o_ready = sem("o_ready")
        mt_done = sem("mt_done")
        o_item, spT_ready = sem("o_item"), sem("spT_ready")
        ssb_done, ssb_read = sem("ssb_done"), sem("ssb_read")
        f1_relu = sem("f1_relu")
        fin_done, fin_first, fin_second = sem("fin_done"), sem("fin_first"), sem("fin_second")
        dve_step, pool_step = sem("dve_step"), sem("pool_step")
        kv_out = sem("kv_out")
        y_out = sem("y_out")

        block = ctx.enter_context(nc.Block())

        GATE_AT = QUARTERS * UU + 1
        POOL_SPLITS = range(S_OUT - 2, S_OUT + NSLOT)
        STEPS_PER_GROUP = 3
        FIN_BANKS = [0, 1, 2, 3, 4, 6, 7]
        NTR = 13
        KV_OUTS = 7

        FIRST_TR = 5 * NT + 1
        TR_AT = {FIRST_TR + i: i for i in range(4)}
        TR_AT.update({FIRST_TR + 8 + 2 * i: 4 + i for i in range(4)})
        TR_AT.update({14 * NT + i: 8 + i for i in range(5)})
        INDEX_AT = [FIRST_TR + 5 + (i // 2 if i < 2 * NIH else i - 2 * NIH // 2) for i in range(NX)]

        def aux_after(n, t):
            g = n * NT + t
            out = [("tr", TR_AT[g])] if g in TR_AT else []
            return out + [("index", i) for i in range(NX) if INDEX_AT[i] == g]

        def last_reader(n):
            l, n = n // SLOTS, n % SLOTS
            if n < S_OUT:
                c, k = divmod(n, QUARTERS)
                return (proj_done, NT * (4 * l + c + 1)) if k == QUARTERS - 1 else (quarter_done, 12 * l + 3 * c + k + 1)
            return unit_done, UNITS * l + n - S_OUT + 1

        def unit_read(u):
            l, u = u // UNITS, u % UNITS
            if u >= KT and (u - KT) % (2 * KT) < KT:
                f = (u - KT) // (2 * KT) * KT + (u - KT) % (2 * KT)
                return f1_relu, FT * l + f + 1
            j = u if u < KT else (u - KT) // (2 * KT) * KT + u % KT + KT
            return y_read, KT * (GROUPS + 1) * l + j + 1

        def raw_use(n):
            return 16 * (n // NRAW + 1)

        @block.sync
        def _(sp):
            row = 0
            for src in (A["norm_mix"], A["norm_ffn"], A["norm_final"], A["b_spatial"]):
                v = src.rearrange("l (k p) -> (l k) p", p=P) if len(src.shape) == 2 else (
                    src.rearrange("(k p) -> k p", p=P) if len(src.shape) == 1 else src.rearrange("l g p -> (l g) p"))
                sp.dma_start(grow[row:row + v.shape[0], :], v).then_inc(const_in, 16)
                row += v.shape[0]

            def load_x(t):
                src = A["x_prompt"][0, t * P:(t + 1) * P, :] if t < NPT else A["x_sample"][0]
                sp.dma_start(x_in[0:ROWS[t], t, :], src).then_inc(x_in_ready[t], 16)

            load_x(0)
            load_x(1)
            for l in range(DEPTH):
                n = [SLOTS * l]

                def load(src, runs):
                    if n[0] >= NRAW:
                        sp.wait_ge(lo_ready, n[0] - NRAW + 1)
                    sp.dma_start(ring_raw[:, n[0] % NRAW, :].rearrange("p (k n) -> p k n", k=runs), src)\
                        .then_inc(w_ready[n[0] % NRAW], 16)
                    n[0] += 1

                for c, c0 in enumerate(CHUNKS):
                    for k in range(QUARTERS):
                        load(A["w_in"][l, k * KQ * P:(k + 1) * KQ * P, c0:c0 + CW]
                             .rearrange("(k p) n -> p k n", p=P), KQ)
                        if n[0] == 1:
                            for t in range(2, NT):
                                load_x(t)
                        if (c, k) == (0, 1):
                            if l:
                                sp.wait_ge(unit_done, UNITS * (l - 1) + 1)
                            sp.dma_start(w_small[:, :, :], A["w_in"][l, :, C_SMALL:C_SMALL + NSM]
                                         .rearrange("(k p) n -> p k n", p=P)).then_inc(ws_in, 16)
                            if l == 0:
                                sp.dma_start(rope_t[:, :, :], A["rope_table"]).then_inc(rope_in, 16)
                    if c == 0:
                        sp.dma_start(cache_k[:, :], A["cache_k"][l, 0].rearrange("s h d -> s (h d)")).then_inc(small_in, 16)
                        sp.dma_start(cache_v[:, :], A["cache_v"][l, 0].rearrange("s h d -> s (h d)")).then_inc(small_in, 16)
                        sp.dma_start(cache_ki[:, :], A["cache_kidx"][l, 0]).then_inc(small_in, 16)
                        sp.dma_start(w_sp[:, :, :], A["w_spatial"][l].rearrange("g i j -> i g j")).then_inc(small_in, 16)
                        sp.dma_start(gate_bc[:, :], A["gate_norm"][l:l + 1, :].broadcast_to([P, DB])).then_inc(small_in, 16)
                for j in range(KT):
                    load(A["w_out"][l, :, j * P:(j + 1) * P].rearrange("(k p) n -> p k n", p=P), KT)
                    if j == 5:
                        sp.wait_ge(roped, l + 1)
                        zp = z[:, 0:NPT, :]
                        zs = z[0:DEC, SMP, :]
                        sp.dma_start(O["k_prompt"][l, 0].rearrange("(t p) h d -> p t (h d)", p=P), zp[:, :, Z_K:Z_K + DKV]).then_inc(kv_out, 16)
                        sp.dma_start(O["v_prompt"][l, 0].rearrange("(t p) h d -> p t (h d)", p=P), zp[:, :, Z_V:Z_V + DKV]).then_inc(kv_out, 16)
                        sp.dma_start(O["kidx_prompt"][l, 0].rearrange("(t p) d -> p t d", p=P), zp[:, :, Z_KI:Z_KI + ID]).then_inc(kv_out, 16)
                        sp.dma_start(O["k_sample"][l, 0].rearrange("p h d -> p (h d)"), zs[:, Z_K:Z_K + DKV]).then_inc(kv_out, 16)
                        sp.dma_start(O["v_sample"][l, 0].rearrange("p h d -> p (h d)"), zs[:, Z_V:Z_V + DKV]).then_inc(kv_out, 16)
                        sp.dma_start(O["kidx_sample"][l, 0], zs[:, Z_KI:Z_KI + ID]).then_inc(kv_out, 16)
                        sp.wait_ge(gvn_ready, NT * l + NT)
                        sp.dma_start(O["gv_sample"][l, 0], gvn[0:DEC, SMP, :]).then_inc(kv_out, 16)
                for g in range(GROUPS):
                    for f in range(KT * g, KT * (g + 1)):
                        load(A["w_ff1"][l, :, f * P:(f + 1) * P].rearrange("(k p) n -> p k n", p=P), KT)
                    for j in range(KT):
                        load(A["w_ff2"][l, g * D:(g + 1) * D, j * P:(j + 1) * P].rearrange("(k p) n -> p k n", p=P), KT)
            for t in range(NT):
                sp.wait_ge(fin_first, t + 1)
                sp.wait_ge(fin_second, t + 1)
                dst = O["y_prompt"][0, t * P:(t + 1) * P, :] if t < NPT else O["y_sample"][0]
                sp.dma_start(dst, out_b[0:ROWS[t], t, :]).then_inc(y_out, 16)
            sp.wait_ge(y_out, 16 * NT)
            sp.wait_ge(kv_out, 16 * KV_OUTS * DEPTH)

        def gain(stage, j):
            c = 2 * DEPTH * KT if stage == 2 * DEPTH else (stage % 2) * DEPTH * KT + stage // 2 * KT
            return gcol[:, c + j:c + j + 1]

        index_parts = [(kih[:, :], kil[:, :], SEQ), (kish[:, :], kisl[:, :], PAST + DEC),
                       (qih[:, 0, P:TOK], qil[:, 0, P:TOK], TOK - P), (qih[:, 1, P:TOK], qil[:, 1, P:TOK], TOK - P)]

        @block.gpsimd
        def _(pool):
            count = [0]

            def link(ins):
                count[0] += 1
                ins.then_inc(pool_step, 1)
                pool.wait_ge(pool_step, count[0])

            g = nc.gpsimd
            link(g.memset(ident[:, :], 0.0))
            g.affine_select(out=ident[:, :], in_=ident[:, :], compare_op=ALU.not_equal, fill=1.0, base=0,
                            pattern=[[-1, P]], channel_multiplier=1).then_inc(const_made, 1)
            g.memset(ones[:, :], 1.0).then_inc(const_made, 1)
            g.memset(ssacc[:, TOK:NT * P], 0.0).then_inc(const_made, 1)
            g.memset(ssv[:, :], 1.0).then_inc(const_made, 1)
            link(g.memset(mask0[:, :], 0.0))
            g.memset(mask0[0:CHUNK, CHUNK:P], OFF).then_inc(const_made, 1)

            def sum_squares(base):
                for j in range(KT):
                    pool.wait_ge(sq_ready, base + j + 1)
                    if j == 0:
                        ins = g.tensor_copy(ssacc[:, 0:TOK], sq[:, j % 2, :])
                    else:
                        pool.wait_ge(ss_added, base + j)
                        ins = g.tensor_tensor(ssacc[:, 0:TOK], ssacc[:, 0:TOK], sq[:, j % 2, :], ALU.add)
                    ins.then_inc(ss_added, 1)

            def newton(y, m):
                link(g.tensor_tensor(nw[:, :], y[:, :], y[:, :], ALU.mult))
                link(g.tensor_tensor(nw[:, :], nw[:, :], m[:, :], ALU.mult))
                link(g.tensor_scalar(nw[:, :], nw[:, :], -0.5, 1.5, ALU.mult, ALU.add))

            def rope(buf, base, heads, width, half, rows, ts, table):
                nt = ts.stop - ts.start
                v = buf[0:rows, ts, base:base + heads * width].rearrange("p t (h d) -> p t h d", h=heads)
                ta = ra[0:rows, ts, 0:heads * 2 * half].rearrange("p t (h d) -> p t h d", h=heads)
                tb = rb[0:rows, ts, 0:heads * 2 * half].rearrange("p t (h d) -> p t h d", h=heads)

                def tab(a, b):
                    return rope_t[0:rows, ts, table + a:table + b].rearrange("p t (o d) -> p t o d", o=1)\
                        .broadcast_to([rows, nt, heads, b - a])
                g.tensor_tensor(ta, v[:, :, :, 0:2 * half], tab(0, 2 * half), ALU.mult)
                g.tensor_tensor(tb[:, :, :, 0:half], v[:, :, :, half:2 * half], tab(2 * half, 3 * half), ALU.mult)
                link(g.tensor_tensor(tb[:, :, :, half:2 * half], v[:, :, :, 0:half], tab(3 * half, 4 * half), ALU.mult))
                return g.tensor_tensor(v[:, :, :, 0:2 * half], ta, tb, ALU.add)

            parts = [(P, slice(0, NPT)), (DEC, slice(SMP, NT))]
            sum_squares(0)
            for l in range(DEPTH):
                pool.wait_ge(root_ready, 2 * l + 1)
                newton(r, ms)
                g.tensor_tensor(r[:, :], r[:, :], nw[:, :], ALU.mult).then_inc(r_ready, 1)
                pool.wait_ge(small_in, 16 * 5 * (l + 1))
                g.tensor_copy(cache_ki4[:, :, :], cache_ki[:, :].rearrange("p (o d) -> p o d", o=1).broadcast_to([P, 4, ID]))
                pool.wait_ge(rope_in, 16)
                pool.wait_ge(small_evac, l + 1)
                pool.wait_ge(proj_evac, 4 * NT * l + NT)
                for rows, ts in parts:
                    link(rope(z, Z_QI, NIH + 1, ID, RI, rows, ts, 4 * RH))
                for rows, ts in parts:
                    g.tensor_copy(ki4[0:rows, ts, :].rearrange("p t (o d) -> p t o d", o=4),
                                  z[0:rows, ts, Z_KI:Z_KI + ID].rearrange("p t (o d) -> p t o d", o=1)
                                  .broadcast_to([rows, ts.stop - ts.start, 4, ID]))
                    last = g.tensor_scalar(wi[0:rows, ts, :], z[0:rows, ts, Z_WI:Z_WI + NIH],
                                           float(ID) ** -0.5 * float(NIH) ** -0.5, None, ALU.mult)
                last.then_inc(idx_roped, 1)
                for rows, ts in parts:
                    last = rope(z, Z_K, NKV, HD, RH, rows, ts, 0)
                last.then_inc(roped, 1)
                def gate_norm():
                    pool.wait_ge(root_ready, 2 * l + 2)
                    newton(rv, mv)
                    g.tensor_tensor(rv[:, :], rv[:, :], nw[:, :], ALU.mult).then_inc(rv_ready, 1)

                for i in range(NX):
                    t, hh = INDEX[i]
                    S, rows = KEYS[t], ROWS[t]
                    pool.wait_ge(scaled, NX * l + i + 1)
                    if hh == 0:
                        ins = g.tensor_copy(score[t][0:rows, :], rl[0:rows, i % 3, 0:S])
                    else:
                        pool.wait_ge(idx_acc, NX * l + i)
                        ins = g.tensor_tensor(score[t][0:rows, :], score[t][0:rows, :], rl[0:rows, i % 3, 0:S], ALU.add)
                    ins.then_inc(idx_acc, 1)
                pool.wait_ge(proj_evac, 4 * NT * l + 2 * NT)
                for rows, ts in parts:
                    last = rope(q, 0, NH, HD, RH, rows, ts, 0)
                last.then_inc(q_roped, 1)
                for n in POOL_SPLITS:
                    if n == S_OUT:
                        gate_norm()
                    pool.wait_ge(lo_ready, SLOTS * l + n)
                    pool.wait_ge(hi_ready, SLOTS * l + n + 1)
                    g.tensor_tensor(ring_lo[:, n % NSLOT, :], ring_raw[:, n % NRAW, :], ring_hi[:, n % NSLOT, :].bitcast(F32),
                                    ALU.subtract).then_inc(lo_ready, 1)
                for a, t in enumerate(TILE_ORDER):
                    pool.wait_ge(proj_evac, 4 * NT * (l + 1))
                    pool.wait_ge(mix_evac, NT * l + a + 1)
                    g.tensor_tensor(ug[0:ROWS[t], t, :], ug[0:ROWS[t], t, :], mb[0:ROWS[t], a % 2, :], ALU.mult)\
                        .then_inc(bm_ready, 1)
                sum_squares(KT * (2 * l + 1))
                sum_squares(KT * (2 * l + 2))
            pool.wait_ge(root_ready, 2 * DEPTH + 1)
            newton(r, ms)
            g.tensor_tensor(r[:, :], r[:, :], nw[:, :], ALU.mult).then_inc(r_ready, 1)

        @block.scalar
        def _(act):
            s = nc.scalar

            def split_hi(n):
                act.wait_ge(w_ready[n % NRAW], raw_use(n))
                if n >= NSLOT:
                    act.wait_ge(*last_reader(n - NSLOT))
                s.activation(ring_hi[:, n % NSLOT, :], ring_raw[:, n % NRAW, :], ACT.Copy).then_inc(hi_ready, 1)

            def feed(j, stage):
                base = KT * stage
                if stage % 2:
                    act.wait_ge(y_read, KT * (GROUPS + 1) * (stage // 2) + j + 1)
                elif stage:
                    act.wait_ge(x_ready, KT * (GROUPS * (stage // 2) - 1) + j + 1)
                else:
                    act.wait_ge(xT_evac, 2 * NT)
                if 0 < stage < 2 * DEPTH:
                    s.activation(xh[:, j, :], x[:, j, :], ACT.Copy, scale=gain(stage, j)).then_inc(xh_ready, 1)
                if base + j >= 2:
                    act.wait_ge(ss_added, base + j - 1)
                s.activation(sq[:, j % 2, :], x[:, j, :], ACT.Square).then_inc(sq_ready, 1)

            for t in range(NT):
                for half in range(2):
                    act.wait_ge(xT_done, 2 * t + half + 1)
                    s.activation(x[:, 4 * half:4 * half + 4, cols(t)],
                                 bank[2 * (t % 2) + half][:, 0:4 * ROWS[t]].rearrange("p (k n) -> p k n", k=4),
                                 ACT.Copy).then_inc(xT_evac, 1)
                if t == 1:
                    split_hi(0)
            act.wait_ge(g_ready, 1)
            for n in range(NSLOT):
                if n:
                    split_hi(n)
                if n == 0:
                    act.wait_ge(xT_evac, 2 * NT)
                for j in (2 * n, 2 * n + 1):
                    s.activation(xh[:, j, :], x[:, j, :], ACT.Copy, scale=gain(0, j)).then_inc(xh_ready, 1)
                for j in (2 * n, 2 * n + 1):
                    feed(j, 0)
            for l in range(DEPTH):
                N0 = SLOTS * l
                def evac(c, t):
                    act.wait_ge(proj_done, NT * (4 * l + c) + t + 1)
                    rows, src = ROWS[t], bank[t]
                    if c == QQ and t == 0:
                        act.wait_ge(small_evac, l + 1)
                    if c == KVQI:
                        dst = z[0:rows, t, 0:CW]
                    elif c == GV:
                        dst = gvn[0:rows, t, :]
                    elif c == UU:
                        dst = ug[0:rows, t, :]
                    if c == QQ:
                        s.activation(q[0:rows, t, :].rearrange("p (b j d) -> p j b d", j=2, d=HD),
                                     src[0:rows, :].rearrange("p (j b d) -> p j b d", j=2, d=HD),
                                     ACT.Copy, scale=r[0:rows, t:t + 1]).then_inc(proj_evac, 1)
                    else:
                        s.activation(dst, src[0:rows, :], ACT.Copy if c == KVQI else ACT.Gelu_apprx_tanh,
                                     scale=r[0:rows, t:t + 1]).then_inc(proj_evac, 1)

                def gating_square(t):
                    act.wait_ge(proj_evac, NT * (4 * l + GV) + t + 1)
                    if t >= 2:
                        act.wait_ge(gv_sq, NT * l + t - 1)
                    s.activation(gsq[0:ROWS[t], t % 2, :], gvn[0:ROWS[t], t, :], ACT.Square,
                                 accum_out=ssv[0:ROWS[t], t:t + 1]).then_inc(gv_sq, 1)

                def index_relu(i):
                    ti, hh = INDEX[i]
                    act.wait_ge(idx_done, NX * l + i + 1)
                    if i >= 3:
                        act.wait_ge(idx_acc, NX * l + i - 2)
                    s.activation(rl[0:ROWS[ti], i % 3, 0:KEYS[ti]], bank[5 + i % 2][0:ROWS[ti], 0:KEYS[ti]],
                                 ACT.Relu).then_inc(idx_relu, 1)

                def index_scale(i):
                    ti, hh = INDEX[i]
                    act.wait_ge(idx_relu, NX * l + i + 1)
                    v = rl[0:ROWS[ti], i % 3, 0:KEYS[ti]]
                    s.activation(v, v, ACT.Copy, scale=wi[0:ROWS[ti], ti, hh:hh + 1]).then_inc(scaled, 1)

                def tr_high(n):
                    act.wait_ge(tr_done, NTR * l + n + 1)
                    dst, width = index_parts[n][0], index_parts[n][2]
                    s.activation(dst, bank[7][:, 0:width], ACT.Copy).then_inc(tr_hi, 1)

                def query_copy(n):
                    act.wait_ge(tr_done, NTR * l + n + 1)
                    if n < 12:
                        out, src = qT[:, n - 8, 0:SEQ], bank[7][:, :]
                    else:
                        out, src = qT[:, :, SEQ:TOK], bank[7][:, 0:4 * DEC].rearrange("p (b n) -> p b n", b=4)
                    s.activation(out, src, ACT.Copy).then_inc(tr_evac, 1)

                for n in range(S_OUT):
                    c, k = divmod(n, QUARTERS)
                    if n:
                        split_hi(N0 + n + NSLOT - 1)
                    if n == 1:
                        act.wait_ge(ws_in, 16 * (l + 1))
                        if l:
                            act.wait_ge(small_done, l)
                        s.activation(w_small_r[:, :, 0, :], w_small[:, :, :], ACT.Copy).then_inc(ws_hi, 1)
                    if n == 2:
                        act.wait_ge(ms_ready, l + 1)
                        s.activation(r[:, :], r[:, :], ACT.Sqrt).then_inc(root_ready, 1)
                        act.wait_ge(r_ready, l + 1)
                    for t in range(NT):
                        if k == QUARTERS - 1:
                            evac(c, t)
                            if c == GV and t:
                                gating_square(t - 1)
                        if n == QUARTERS * UU and t == 0:
                            gating_square(NT - 1)
                        if n == GATE_AT and t == 1:
                            act.wait_ge(mv_ready, l + 1)
                            s.activation(rv[:, :], rv[:, :], ACT.Sqrt).then_inc(root_ready, 1)
                        for kind, i in aux_after(n, t):
                            if kind == "index":
                                index_relu(i)
                                if i:
                                    index_scale(i - 1)
                                if i == NX - 1:
                                    index_scale(i)
                            elif i < 4:
                                tr_high(i)
                            elif i >= 8:
                                query_copy(i)
                split_hi(N0 + S_OUT + NSLOT - 1)

                def exp(i):
                    t, hh = ITEMS[i]
                    act.wait_ge(masked, NI * l + i + 1)
                    if i >= 2:
                        act.wait_ge(pT_done, NI * l + i - 1)
                    s.activation(pr[0:ROWS[t], i % 2, 0:KEYS[t]], L[0:ROWS[t], i % 3, 0:KEYS[t]], ACT.Exp,
                                 scale=-1.0, bias=nmax[0:ROWS[t], i:i + 1],
                                 accum_out=rsum[0:ROWS[t], i:i + 1]).then_inc(exp_done, 1)

                def pT_copy(i):
                    t, hh = ITEMS[i]
                    act.wait_ge(pT_done, NI * l + i + 1)
                    if i >= 2:
                        act.wait_ge(o_item, NI * l + i - 1)
                    n = -(-KEYS[t] // P) * ROWS[t]
                    if t == SMP:
                        s.activation(pT[:, i % 2, 0:DEC], bank[2 + i % 2][:, 0:DEC], ACT.Copy)
                        s.activation(pT[0:DEC, i % 2, DEC:2 * DEC], bank[2 + i % 2][0:DEC, DEC:2 * DEC],
                                     ACT.Copy).then_inc(pT_evac, 1)
                    else:
                        s.activation(pT[:, i % 2, 0:n], bank[2 + i % 2][:, 0:n], ACT.Copy).then_inc(pT_evac, 1)

                def mt_copy(a, part):
                    t, pos = TILE_ORDER[a], part if a < NT - 1 else 1 - part
                    act.wait_ge(mt_done, 2 * NT * l + 2 * a + pos + 1)
                    k0 = 0 if part == 0 else KT // 2
                    s.activation(vh[:, k0:k0 + 4, cols(t)], bank[7 - part][:, 0:4 * ROWS[t]].rearrange("p (k n) -> p k n", k=4),
                                 ACT.Copy).then_inc(vh_ready, 1)

                exp(0)
                act.wait_ge(idx_acc, NX * (l + 1))
                for i in range(NI):
                    if i + 1 < NI:
                        exp(i + 1)
                    pT_copy(i)
                    if i % NH == 5 and i > NH:
                        mt_copy(i // NH - 1, 0)
                        mt_copy(i // NH - 1, 1)
                mt_copy(NT - 1, 1)
                mt_copy(NT - 1, 0)
                for j in range(KT):
                    feed(j, 2 * l + 1)
                    split_hi(N0 + S_OUT + j + NSLOT)
                for u in range(KT, UNITS):
                    g, f = divmod(u - KT, 2 * KT)
                    if f < KT:
                        f += KT * g
                        act.wait_ge(unit_done, UNITS * l + u + 1)
                        if f >= 2:
                            act.wait_ge(vl_ready, (2 * NT + FT) * l + 2 * NT + f - 1)
                        for half in range(2):
                            last = s.activation(rl2[:, f % 2, HALVES[half]], bank[2 * (u % 4) + half][:, 0:HALF], ACT.Relu)
                        last.then_inc(f1_relu, 1)
                        act.wait_ge(f1_relu, FT * l + f + 1)
                        s.activation(vh[:, f % KT, :], rl2[:, f % 2, :], ACT.Square).then_inc(vh_ready, 1)
                    elif g == GROUPS - 1:
                        feed(u % KT, 2 * l + 2)
                    if l < DEPTH - 1 or u < UNITS - NSLOT:
                        split_hi(N0 + S_OUT + u + NSLOT)
            act.wait_ge(ms_ready, DEPTH + 1)
            s.activation(r[:, :], r[:, :], ACT.Sqrt).then_inc(root_ready, 1)
            act.wait_ge(r_ready, DEPTH + 1)
            for t in range(NT):
                act.wait_ge(fin_done, 2 * t + 1)
                s.activation(out_b[0:ROWS[t], t, 0:CW], bank[FIN_BANKS[2 * t % 7]][0:ROWS[t], :], ACT.Copy,
                             scale=r[0:ROWS[t], t:t + 1]).then_inc(fin_first, 1)

        @block.vector
        def _(dve):
            v = nc.vector
            count = [0]

            def link(ins):
                count[0] += 1
                ins.then_inc(dve_step, 1)
                dve.wait_ge(dve_step, count[0])

            def split_lo(n):
                dve.wait_ge(hi_ready, n + 1)
                v.tensor_tensor(ring_lo[:, n % NSLOT, :], ring_raw[:, n % NRAW, :], ring_hi[:, n % NSLOT, :].bitcast(F32),
                                ALU.subtract).then_inc(lo_ready, 1)

            def feed(j, base, stage):
                dve.wait_ge(xh_ready, base + j + 1)
                v.scalar_tensor_tensor(xl[:, j, :], x[:, j, :], gain(stage, j), xh[:, j, :].bitcast(F32),
                                       ALU.mult, ALU.subtract).then_inc(xl_ready, 1)

            def last_gain(j):
                dve.wait_ge(sq_ready, KT * 2 * DEPTH + j + 1)
                v.tensor_scalar(x[:, j, :], x[:, j, :], gain(2 * DEPTH, j), None, ALU.mult).then_inc(y_scaled, 1)

            def row_mean(n):
                dve.wait_ge(ss_done, n + 1)
                link(v.tensor_scalar(ms[:, :], bank[5][:, 0:NT], 1.0 / D, EPS, ALU.mult, ALU.add))
                v.reciprocal(r[:, :], ms[:, :]).then_inc(ms_ready, 1)

            dve.wait_ge(gT_done, 1)
            v.tensor_copy(gcol[:, :], bank[7][:, 0:7 * KT]).then_inc(g_ready, 1)
            dve.wait_ge(g_ready, 1)
            for n in range(NSLOT):
                split_lo(n)
                feed(2 * n, 0, 0)
                feed(2 * n + 1, 0, 0)
            for l in range(DEPTH):
                N0 = SLOTS * l
                def small_copy():
                    dve.wait_ge(r_ready, l + 1)
                    dve.wait_ge(small_tr, l + 1)
                    src = bank[5][:, 0:NT * 2 * NSM].rearrange("p (t a n) -> p t a n", t=NT, a=2)
                    for k in range(2):
                        for rows, ts in ((P, slice(0, NPT)), (DEC, slice(SMP, NT))):
                            nt = ts.stop - ts.start
                            rr = r[0:rows, ts].rearrange("p (t o) -> p t o", o=1).broadcast_to([rows, nt, NSM])
                            dst = z[0:rows, ts, CW:ZW] if k == 0 else zs2[0:rows, ts, :]
                            last = v.tensor_tensor(dst, src[0:rows, ts, k, :], rr, ALU.mult)
                    link(last)
                    for rows, ts in ((P, slice(0, NPT)), (DEC, slice(SMP, NT))):
                        last = v.tensor_tensor(z[0:rows, ts, CW:ZW], z[0:rows, ts, CW:ZW], zs2[0:rows, ts, :], ALU.add)
                    last.then_inc(small_evac, 1)

                dst = [kT, kTs]
                width = [SEQ, PAST + DEC]

                def tr_copy(n):
                    dve.wait_ge(tr_done, NTR * l + n + 1)
                    if n < 4:
                        dve.wait_ge(tr_hi, 4 * l + n + 1)
                        hi, lo, w = index_parts[n]
                        v.tensor_tensor(lo, bank[7][:, 0:w], hi.bitcast(F32), ALU.subtract).then_inc(tr_evac, 1)
                        return
                    if n < 6:
                        out, src = dst[n - 4], bank[7][:, 0:width[n - 4]]
                    else:
                        k = 4 * (n - 6)
                        out, src = w_spT[:, k:k + 4, :], bank[7][:, :].rearrange("p (g n) -> p g n", g=4)
                    v.tensor_copy(out, src).then_inc(tr_evac, 1)
                    if n == 7:
                        dve.wait_ge(tr_evac, NTR * l + 8)
                        v.memset(w_spT[CHUNK:P, :, 0:CHUNK], 0.0).then_inc(spT_ready, 1)

                done = {t: 0 for t in INDEX_TILES}
                step_of = {}

                def total_steps(t):
                    return 1 + 2 * (TOP_S if t == SMP else TOP_P) // 8 + 1

                def topk_step(t):
                    rows, n, sc = ROWS[t], done[t], score[t]
                    m = m8[0:rows, INDEX_TILES.index(t), :]
                    if n == 0:
                        dve.wait_ge(idx_acc, NX * l + NIH * (INDEX_TILES.index(t) + 1))
                        if t == SMP:
                            done[t] = 1
                            return
                        ins = v.memset(sc[0:CHUNK, KEYS[t] - CHUNK:KEYS[t]], NEG)
                    else:
                        if t in step_of:
                            dve.wait_ge(dve_step, step_of[t])
                        if n == total_steps(t) - 1:
                            ins = v.tensor_scalar(sc[0:rows, :], sc[0:rows, :], SPLIT, OFF, ALU.is_gt, ALU.mult)
                        elif n % 2:
                            ins = v.max(m, sc[0:rows, :])
                        else:
                            ins = v.match_replace(sc[0:rows, :], m, sc[0:rows, :], TAKEN)
                    count[0] += 1
                    ins.then_inc(dve_step, 1)
                    step_of[t] = count[0]
                    done[t] += 1

                turn = [0]

                def topk_next(g):
                    ready = [t for t in INDEX_TILES if done[t] < total_steps(t) and
                             (done[t] or g >= INDEX_AT[NIH * INDEX_TILES.index(t) + NIH - 1] + 3)][:2]
                    if ready:
                        topk_step(ready[turn[0] % len(ready)])
                        turn[0] += 1

                def masked_logits(i):
                    t, hh = ITEMS[i]
                    rows, S = ROWS[t], KEYS[t]
                    dve.wait_ge(qk_done, NI * l + i + 1)
                    if i >= 3:
                        dve.wait_ge(exp_done, NI * l + i - 2)
                    mk = mask0[0:rows, :] if t == 0 else score[t][0:rows, :]
                    v.tensor_tensor_reduce(out=L[0:rows, i % 3, 0:S], in0=bank[i % 2][0:rows, 0:S], in1=mk,
                                           scale=-SCALE, scalar=3e38, op0=ALU.add, op1=ALU.min,
                                           accum_out=nmax[0:rows, i:i + 1]).then_inc(masked, 1)

                def gv_norm(t):
                    v.scalar_tensor_tensor(gvn[0:ROWS[t], t, :], gvn[0:ROWS[t], t, :], rv[0:ROWS[t], t:t + 1],
                                           gate_bc[0:ROWS[t], :], ALU.mult, ALU.mult).then_inc(gvn_ready, 1)

                def mix_copy(a):
                    t = TILE_ORDER[a]
                    dve.wait_ge(mix_done, NT * l + a + 1)
                    if a >= 2:
                        dve.wait_ge(bm_ready, NT * l + a - 1)
                    c0 = (2 * DEPTH + 1) * KT + l * NG
                    v.tensor_tensor(mb[0:ROWS[t], a % 2, :].rearrange("p (g c) -> p g c", g=NG),
                                    bank[6][0:ROWS[t], :].rearrange("p (g c) -> p g c", g=NG),
                                    gcol[0:ROWS[t], c0:c0 + NG].rearrange("p (g o) -> p g o", o=1)
                                    .broadcast_to([ROWS[t], NG, CPG]), ALU.add).then_inc(mix_evac, 1)

                def o_copy(a):
                    t = TILE_ORDER[a]
                    rows = ROWS[t]
                    dve.wait_ge(o_item, NI * l + NH * (a + 1))
                    link(v.reciprocal(rinv[0:rows, NH * a:NH * (a + 1)], rsum[0:rows, NH * a:NH * (a + 1)]))
                    v.tensor_tensor(o[0:rows, a % 2, :].rearrange("p (h d) -> p h d", h=NH),
                                    bank[4 + a % 2][0:rows, :].rearrange("p (h d) -> p h d", h=NH),
                                    rinv[0:rows, NH * a:NH * (a + 1)].rearrange("p (h o) -> p h o", o=1)
                                    .broadcast_to([rows, NH, HD]), ALU.mult).then_inc(o_ready, 1)

                def mt_low(a, part):
                    t = TILE_ORDER[a]
                    pos = part if a < NT - 1 else 1 - part
                    dve.wait_ge(vh_ready, (2 * NT + FT) * l + 2 * a + pos + 1)
                    k0 = 0 if part == 0 else KT // 2
                    v.tensor_tensor(vl[:, k0:k0 + 4, cols(t)], bank[7 - part][:, 0:4 * ROWS[t]].rearrange("p (k n) -> p k n", k=4),
                                    vh[:, k0:k0 + 4, cols(t)].bitcast(F32), ALU.subtract).then_inc(vl_ready, 1)

                for n in range(S_OUT):
                    if n and n + NSLOT - 1 not in POOL_SPLITS:
                        split_lo(N0 + n + NSLOT - 1)
                    if n == 2:
                        row_mean(l)
                        dve.wait_ge(ws_hi, l + 1)
                        v.tensor_tensor(w_small_r[:, :, 1, :], w_small[:, :, :], w_small_r[:, :, 0, :].bitcast(F32),
                                        ALU.subtract).then_inc(ws_split, 1)
                    if n == QUARTERS:
                        dve.wait_ge(small_done, l + 1)
                        for half in range(2):
                            last = v.tensor_copy(small_fm[0:2 * NSM, HALVES[half]], bank[6 + half][0:2 * NSM, 0:HALF])
                        last.then_inc(small_fm_ready, 1)
                        small_copy()
                    for t in range(NT):
                        for kind, i in aux_after(n, t):
                            if kind == "tr" and i < 8:
                                tr_copy(i)
                        g = n * NT + t
                        if n == GATE_AT and t == 0:
                            dve.wait_ge(gv_sq, NT * (l + 1))
                            link(v.tensor_scalar(mv[:, :], ssv[:, :], 1.0 / DB, EPS, ALU.mult, ALU.add))
                            v.reciprocal(rv[:, :], mv[:, :]).then_inc(mv_ready, 1)
                        if n == GATE_AT + 2 and t == 2:
                            dve.wait_ge(rv_ready, l + 1)
                            gv_norm(TILE_ORDER[0])
                            continue
                        for _ in range(STEPS_PER_GROUP):
                            topk_next(g)
                left = sum(total_steps(t) - done[t] for t in INDEX_TILES)
                before = [KEYS[t] + P for t, _ in ITEMS[:(NT - 1) * NH]]
                for i in range(NI):
                    a, t = i // NH, ITEMS[i][0]
                    if i % NH == 0 and t:
                        while done[t] < total_steps(t):
                            topk_next(S_OUT * NT)
                        dve.wait_ge(dve_step, step_of[t])
                    while left - sum(total_steps(t_) - done[t_] for t_ in INDEX_TILES) < left * min(1, sum(before[:i + 1]) / sum(before)):
                        topk_next(S_OUT * NT)
                    masked_logits(i)
                    if i % NH == 1 and a + 1 < NT:
                        gv_norm(TILE_ORDER[a + 1])
                    if i % NH == 3 and a:
                        o_copy(a - 1)
                    if i % NH == 6:
                        mix_copy(a)
                    if i % NH == 7 and a:
                        mt_low(a - 1, 0)
                        mt_low(a - 1, 1)
                mt_low(NT - 1, 1)
                o_copy(NT - 1)
                mt_low(NT - 1, 0)
                for j in range(KT):
                    dve.wait_ge(unit_done, UNITS * l + j + 1)
                    b = 2 * (j % 4)
                    for half in range(2):
                        last = v.tensor_tensor(x[:, j, HALVES[half]], x[:, j, HALVES[half]], bank[b + half][:, 0:HALF], ALU.add)
                    last.then_inc(y_read, 1)
                    if j:
                        feed(j - 1, KT * (2 * l + 1), 2 * l + 1)
                    if j == 0:
                        dve.wait_ge(lo_ready, N0 + S_OUT + NSLOT)
                    split_lo(N0 + S_OUT + j + NSLOT)
                feed(KT - 1, KT * (2 * l + 1), 2 * l + 1)
                for u in range(KT, UNITS):
                    g, f = divmod(u - KT, 2 * KT)
                    b = 2 * (u % 4)
                    if f < KT:
                        f += KT * g
                        if f == 0:
                            dve.wait_ge(kv_out, 16 * KV_OUTS * (l + 1))
                        dve.wait_ge(f1_relu, FT * l + f + 1)
                        link(v.tensor_tensor(h32[:, f % 2, :], rl2[:, f % 2, :], rl2[:, f % 2, :], ALU.mult))
                        dve.wait_ge(vh_ready, (2 * NT + FT) * l + 2 * NT + f + 1)
                        v.tensor_tensor(vl[:, f % KT, :], h32[:, f % 2, :], vh[:, f % KT, :].bitcast(F32), ALU.subtract)\
                            .then_inc(vl_ready, 1)
                    else:
                        j = f - KT
                        n = KT * (GROUPS * l + g) + j
                        dve.wait_ge(unit_done, UNITS * l + u + 1)
                        for half in range(2):
                            last = v.tensor_tensor(yb[:, j % 2, HALVES[half]], r2b[:, HALVES[half]], bank[b + half][:, 0:HALF],
                                                   ALU.mult)
                        last.then_inc(y_read, 1)
                        dve.wait_ge(y_read, KT * (GROUPS + 1) * l + KT * (g + 1) + j + 1)
                        v.tensor_tensor(x[:, j, :], x[:, j, :], yb[:, j % 2, :], ALU.add).then_inc(x_ready, 1)
                        if g == GROUPS - 1 and j and l == DEPTH - 1:
                            last_gain(j - 1)
                        elif g == GROUPS - 1 and j:
                            feed(j - 1, KT * (2 * l + 2), 2 * l + 2)
                    if l < DEPTH - 1 or u < UNITS - NSLOT:
                        split_lo(N0 + S_OUT + u + NSLOT)
                    if u == KT + 1:
                        dve.wait_ge(ssb_done, l + 1)
                        for half in range(2):
                            last = v.tensor_scalar(r2b[:, HALVES[half]], bank[6 + half][:, 0:HALF], 1.0 / D, EPS,
                                                   ALU.mult, ALU.add)
                        last.then_inc(ssb_read, 1)
                        dve.wait_ge(ssb_read, l + 1)
                        link(v.reciprocal(r2b[:, :], r2b[:, :]))
                if l < DEPTH - 1:
                    feed(KT - 1, KT * (2 * l + 2), 2 * l + 2)
            last_gain(KT - 1)
            row_mean(DEPTH)
            dve.wait_ge(r_ready, DEPTH + 1)
            for t in range(NT):
                dve.wait_ge(fin_done, 2 * t + 2)
                v.tensor_scalar(out_b[0:ROWS[t], t, CW:2 * CW], bank[FIN_BANKS[(2 * t + 1) % 7]][0:ROWS[t], :],
                                r[0:ROWS[t], t:t + 1], None, ALU.mult).then_inc(fin_second, 1)

        @block.tensor
        def _(pe):
            mm = nc.tensor.matmul
            tp = nc.tensor.transpose

            def row_sums(n):
                pe.wait_ge(ss_added, KT * (2 * n + 1))
                for t in range(NT):
                    last = mm(bank[5][:, t:t + 1], ssacc[:, t * P:(t + 1) * P], ones[:, 0:1], start=True, stop=True)
                last.then_inc(ss_done, 1)

            pe.wait_ge(const_made, 5)
            pe.wait_ge(const_in, 16 * 4)
            tp(bank[7][:, 0:7 * KT], grow[:, :], ident[0:7 * KT, 0:7 * KT]).then_inc(gT_done, 1)
            for t in range(NT):
                pe.wait_ge(x_in_ready[t], 16)
                for half in range(2):
                    if t >= 2:
                        pe.wait_ge(xT_evac, 2 * t + half - 3)
                    for k in range(4):
                        last = tp(bank[2 * (t % 2) + half][:, k * ROWS[t]:(k + 1) * ROWS[t]],
                                  x_in[0:ROWS[t], t, (4 * half + k) * P:(4 * half + k + 1) * P],
                                  ident[0:ROWS[t], 0:ROWS[t]])
                    last.then_inc(xT_done, 1)

            for l in range(DEPTH):
                def slot(n):
                    pe.wait_ge(lo_ready, SLOTS * l + n + 1)
                    return tuple(b[:, n % NSLOT, :] for b in (ring_hi, ring_lo))

                def group(n, t, w):
                    c, k = divmod(n, QUARTERS)
                    if k == 0 and c:
                        pe.wait_ge(proj_evac, NT * (4 * l + c - 1) + t + 1)
                    elif n == 0 and l:
                        pe.wait_ge(*unit_read(UNITS * l - 4 + t // 2))
                    wh, wl = (b.rearrange("p (k n) -> p k n", k=KQ) for b in w)
                    for kk in range(KQ):
                        kx = KQ * k + kk
                        for a, b in ((xh, wh), (xh, wl), (xl, wh)):
                            last = mm(bank[t][0:ROWS[t], :], a[:, kx, cols(t)], b[:, kk, :],
                                      start=kx == 0 and b is wh and a is xh, stop=kx == KT - 1 and a is xl)
                    if k == QUARTERS - 1:
                        last.then_inc(proj_done, 1)
                    elif t == NT - 1:
                        last.then_inc(quarter_done, 1)

                def index(i):
                    t, hh = INDEX[i]
                    if i == 0:
                        pe.wait_ge(tr_evac, NTR * l + 4)
                    if i >= 2:
                        pe.wait_ge(idx_relu, NX * l + i - 1)
                    b, rows = 32 * (hh % 4), ROWS[t]
                    kh, kl = (kish, kisl) if t == SMP else (kih, kil)
                    for a, k in ((qih, kh), (qih, kl), (qil, kh)):
                        last = mm(bank[5 + i % 2][0:rows, 0:KEYS[t]], a[b:b + ID, hh // 4, cols(t)], k[b:b + ID, 0:KEYS[t]],
                                  start=a is qih and k is kh, stop=a is qil)
                    last.then_inc(idx_done, 1)

                tr = [0]

                def tr_group(parts):
                    n = NTR * l + tr[0]
                    if n:
                        pe.wait_ge(tr_evac, n)
                    c0 = 0
                    for src in parts:
                        rows = src.shape[0]
                        last = tp(bank[7][:, c0:c0 + rows], src, ident[0:rows, 0:rows])
                        c0 += rows
                    last.then_inc(tr_done, 1)
                    tr[0] += 1

                zz = lambda t, a, b: z[0:ROWS[t], t, a:b]
                tr_parts = [[ki4[:, t, :] for t in range(NPT)],
                            [cache_ki4[:, :, :].rearrange("p a d -> p (a d)"), ki4[0:DEC, SMP, :]]]
                tr_parts += [[zz(t, Z_QI + b * P, Z_QI + (b + 1) * P) for t in list(range(1, NPT)) + [SMP]] for b in range(2)]
                tr_parts += [[zz(t, Z_K, Z_K + DKV) for t in range(NPT)],
                             [cache_k[:, :], zz(SMP, Z_K, Z_K + DKV)]]
                tr_parts += [[w_sp[:, 4 * n + g, :] for g in range(4)] for n in range(2)]
                tr_parts += [[q[:, t, b * P:(b + 1) * P] for t in range(NPT)] for b in range(4)]
                tr_parts += [[q[0:DEC, SMP, b * P:(b + 1) * P] for b in range(4)]]

                for n in range(S_OUT):
                    w = slot(n)
                    if n < QUARTERS:
                        pe.wait_ge(xl_ready, KT * 2 * l + KQ * (n + 1))
                    for t in range(NT):
                        group(n, t, w)
                        if n == QUARTERS and t == 0:
                            pe.wait_ge(small_fm_ready, l + 1)
                            for tt in range(NT):
                                last = tp(bank[5][0:ROWS[tt], 2 * NSM * tt:2 * NSM * (tt + 1)], small_fm[0:2 * NSM, cols(tt)],
                                          ident[0:2 * NSM, 0:2 * NSM])
                            last.then_inc(small_tr, 1)
                        for kind, i in aux_after(n, t):
                            if kind == "tr":
                                if i == 0:
                                    pe.wait_ge(small_in, 16 * 5 * (l + 1))
                                    pe.wait_ge(idx_roped, l + 1)
                                if i == 4:
                                    pe.wait_ge(roped, l + 1)
                                if i == 8:
                                    pe.wait_ge(q_roped, l + 1)
                                tr_group(tr_parts[i])
                            else:
                                index(i)
                    if n == 1:
                        row_sums(l)
                    if n == QUARTERS - 1:
                        pe.wait_ge(ws_split, l + 1)
                        pe.wait_ge(ms_ready, l + 1)
                        for half in range(2):
                            for k in range(KT):
                                both = w_small_r[:, k, :, :].rearrange("p a n -> p (a n)")
                                high = w_small_r[:, k, 0, :]
                                steps = [(both, xh, 2 * NSM), (high, xl, NSM)]
                                if k == KT - 1:
                                    steps = steps[::-1]
                                for m, (w_, a_, n_) in enumerate(steps):
                                    last = mm(bank[6 + half][0:n_, 0:HALF], w_, a_[:, k, HALVES[half]],
                                              start=k == 0 and m == 0, stop=k == KT - 1 and m == 1)
                        last.then_inc(small_done, 1)

                def scores_of(i):
                    t, hh = ITEMS[i]
                    if i == 0:
                        pe.wait_ge(tr_evac, NTR * (l + 1))
                        pe.wait_ge(idx_relu, NX * (l + 1))
                    if i < 2:
                        pe.wait_ge(proj_evac, 4 * NT * l + 3 * NT + 1 + i)
                    if i >= 2:
                        pe.wait_ge(masked, NI * l + i - 1)
                    b = HD * (hh // 4)
                    keys = kTs if t == SMP else kT
                    mm(bank[i % 2][0:ROWS[t], 0:KEYS[t]], qT[b:b + HD, hh % 4, cols(t)], keys[b:b + HD, 0:KEYS[t]],
                       start=True, stop=True).then_inc(qk_done, 1)

                def p_transpose(i):
                    t, hh = ITEMS[i]
                    pe.wait_ge(exp_done, NI * l + i + 1)
                    if i < 2:
                        pe.wait_ge(proj_evac, 4 * NT * l + 3 * NT + 3 + i)
                    if i >= 2:
                        pe.wait_ge(pT_evac, NI * l + i - 1)
                    for s0 in range(0, KEYS[t], P):
                        n = min(P, KEYS[t] - s0)
                        c0 = s0 // P * ROWS[t]
                        last = tp(bank[2 + i % 2][0:n, c0:c0 + ROWS[t]], pr[0:ROWS[t], i % 2, s0:s0 + n],
                                  ident[0:ROWS[t], 0:ROWS[t]])
                    last.then_inc(pT_done, 1)

                def weighted(i):
                    t, hh = ITEMS[i]
                    a = i // NH
                    pe.wait_ge(pT_evac, NI * l + i + 1)
                    if hh == 0 and a >= 2:
                        pe.wait_ge(o_ready, NT * l + a - 1)
                    nb = -(-KEYS[t] // P)
                    g0 = Z_V + HD * (hh // 4)
                    for s in range(nb):
                        n = min(P, KEYS[t] - s * P)
                        if t == SMP:
                            vals = cache_v[:, HD * (hh // 4):HD * (hh // 4) + HD] if s == 0 else z[0:DEC, SMP, g0:g0 + HD]
                        else:
                            vals = z[:, s, g0:g0 + HD]
                        last = mm(bank[4 + a % 2][0:ROWS[t], hh * HD:(hh + 1) * HD],
                                  pT[0:n, i % 2, s * ROWS[t]:(s + 1) * ROWS[t]], vals, start=s == 0, stop=s == nb - 1)
                    last.then_inc(o_item, 1)

                def spatial(a):
                    t = TILE_ORDER[a]
                    pe.wait_ge(spT_ready, l + 1)
                    pe.wait_ge(gvn_ready, NT * l + a + 1)
                    if a >= 2:
                        pe.wait_ge(vl_ready, (2 * NT + FT) * l + 2 * (a - 1))
                    rows = ROWS[t]
                    for g in range(NG):
                        last = mm(bank[6][0:rows, g * CPG:(g + 1) * CPG], w_spT[0:rows, g, 0:rows],
                                  gvn[0:rows, t, g * CPG:(g + 1) * CPG], start=True, stop=True)
                    last.then_inc(mix_done, 1)

                def mt_group(a, part):
                    t = TILE_ORDER[a]
                    if a:
                        pe.wait_ge(vl_ready, (2 * NT + FT) * l + 2 * a)
                    if part:
                        pe.wait_ge(mix_evac, NT * l + min(a + 2, NT))
                    pe.wait_ge(o_ready if part == 0 else bm_ready, NT * l + a + 1)
                    src = o[0:ROWS[t], a % 2, :] if part == 0 else ug[0:ROWS[t], t, :]
                    for k in range(4):
                        last = tp(bank[7 - part][:, k * ROWS[t]:(k + 1) * ROWS[t]], src[:, k * P:(k + 1) * P],
                                  ident[0:ROWS[t], 0:ROWS[t]])
                    last.then_inc(mt_done, 1)

                scores_of(0)
                scores_of(1)
                spatial(0)
                for i in range(NI):
                    if i % NH == 4 and i > NH:
                        spatial(i // NH)
                    if i + 2 < NI:
                        scores_of(i + 2)
                    p_transpose(i)
                    if i:
                        weighted(i - 1)
                    if i % NH == 5 and i > NH:
                        mt_group(i // NH - 1, 0)
                        mt_group(i // NH - 1, 1)
                mt_group(NT - 1, 1)
                weighted(NI - 1)
                mt_group(NT - 1, 0)
                pe.wait_ge(vl_ready, (2 * NT + FT) * l + 2 * NT - 1)
                for u in range(UNITS):
                    wh, wl = (b.rearrange("p (k n) -> p k n", k=KT) for b in slot(S_OUT + u))
                    g, f = divmod(u - KT, 2 * KT)
                    first_product = u >= KT and f < KT
                    ah, al = (xh, xl) if first_product else (vh, vl)
                    if u >= 4:
                        pe.wait_ge(*unit_read(UNITS * l + u - 4))
                    if u == KT + 3:
                        pe.wait_ge(ssb_read, l + 1)
                    order = list(range(KT)) if u >= KT else list(range(KT // 2, KT)) + list(range(KT // 2))
                    for k in order:
                        if u == 0 and k == 0:
                            pe.wait_ge(vl_ready, (2 * NT + FT) * l + 2 * NT)
                        if u == KT:
                            pe.wait_ge(xl_ready, KT * (2 * l + 1) + k + 1)
                        if u >= KT and f == KT:
                            pe.wait_ge(vl_ready, (2 * NT + FT) * l + 2 * NT + KT * g + k + 1)
                        for w, a in ((wh, ah), (wh, al), (wl, ah)):
                            for half in range(2):
                                last = mm(bank[2 * (u % 4) + half][:, 0:HALF], w[:, k, :], a[:, k, HALVES[half]],
                                          start=k == order[0] and w is wh and a is ah, stop=k == order[-1] and w is wl)
                    last.then_inc(unit_done, 1)
                    if u == KT + 1:
                        pe.wait_ge(ss_added, KT * (2 * l + 2))
                        for half in range(2):
                            last = mm(bank[6 + half][:, 0:HALF], ones[:, :], ssacc[:, HALVES[half]], start=True, stop=True)
                        last.then_inc(ssb_done, 1)
            pe.wait_ge(y_scaled, KT)
            row_sums(DEPTH)
            for t in range(NT):
                for half in range(2):
                    n = 2 * t + half
                    if n >= 7:
                        pe.wait_ge((fin_first, fin_second)[(n - 7) % 2], (n - 7) // 2 + 1)
                    for k in range(4):
                        last = tp(bank[FIN_BANKS[n % 7]][0:ROWS[t], k * P:(k + 1) * P], x[:, 4 * half + k, cols(t)], ident[:, :])
                    last.then_inc(fin_done, 1)


_INS = ['x_prompt', 'x_sample', 'cache_k', 'cache_v', 'cache_kidx', 'norm_mix', 'w_in', 'gate_norm', 'w_spatial',
        'b_spatial', 'w_out', 'norm_ffn', 'w_ff1', 'w_ff2', 'norm_final']


def kernel(**inputs):
    import concourse.bacc as bacc
    from concourse import mybir
    from concourse.bass_utils import run_bass_kernel_spmd

    nc = bacc.Bacc("TRN2", target_bir_lowering=False, num_devices=1)
    arrays = {n: np.ascontiguousarray(inputs[n]) for n in _INS}
    L, B, past, nkv, hd = arrays['cache_k'].shape
    seq, d = arrays['x_prompt'].shape[1:]
    dec = arrays['x_sample'].shape[1]
    idd = arrays['cache_kidx'].shape[3]
    db = arrays['gate_norm'].shape[1]

    nt = seq // 128 + 1
    pos = np.arange(nt * 128).reshape(nt, 128).T.astype(np.float32)
    pos[:, nt - 1] = past + np.arange(128)
    parts = []
    for half in (hd // 8, idd // 8):
        inv = np.power(np.float32(500000.0), -np.arange(half, dtype=np.float32) * np.float32(2.0 / (2 * half)))
        ang = (pos[:, :, None] * inv.astype(np.float32)).astype(np.float32)
        c, s = np.cos(ang), np.sin(ang)
        parts += [c, c, -s, s]
    arrays['rope_table'] = np.concatenate(parts, -1).astype(np.float32)

    outs = {'y_prompt': (B, seq, d), 'y_sample': (B, dec, d), 'k_prompt': (L, B, seq, nkv, hd),
            'v_prompt': (L, B, seq, nkv, hd), 'kidx_prompt': (L, B, seq, idd), 'k_sample': (L, B, dec, nkv, hd),
            'v_sample': (L, B, dec, nkv, hd), 'kidx_sample': (L, B, dec, idd), 'gv_sample': (L, B, dec, db)}
    A = {n: nc.dram_tensor(f"in_{n}", a.shape, mybir.dt.from_np(a.dtype), kind="ExternalInput").ap()
         for n, a in arrays.items()}
    O = {n: nc.dram_tensor(f"out_{n}", s, mybir.dt.float32, kind="ExternalOutput").ap() for n, s in outs.items()}
    hybrid_encoder_program(nc, A, O)
    res = run_bass_kernel_spmd(nc, [{f"in_{n}": a for n, a in arrays.items()}], core_ids=[0])
    return tuple(res.results[0][f"out_{n}"] for n in outs)
```
